# Optimizing a Trainium2 kernel written in Bass

```python
import jax, jax.numpy as jnp
from jax import lax
import numpy as np

D_MODEL = 1024
BATCH = 1
SEQ = 256
DEPTH = 2

N_HEADS = 16
HEAD_DIM = D_MODEL // N_HEADS
N_KV_HEADS = 4
GROUP = N_HEADS // N_KV_HEADS
ROT_DIM = HEAD_DIM // 4
ROPE_THETA = 500000.0
WINDOW = 128
BLOCK = 128
CONV_WIDTH = D_MODEL
CONV_K = 3
D_FF = -(-8 * D_MODEL // (3 * 256)) * 256
Q_W = N_HEADS * HEAD_DIM
KV_W = N_KV_HEADS * HEAD_DIM
IN_COLS = Q_W + 2 * KV_W + 3 * CONV_WIDTH + 2 * D_MODEL
RMS_EPS = 1e-6
NEG_INF = -1e30


def rms_norm(x, g):
    xf = x.astype(jnp.float32)
    y = xf * lax.rsqrt(jnp.mean(xf * xf, axis=-1, keepdims=True) + RMS_EPS)
    return (y * g.astype(jnp.float32)).astype(x.dtype)

def rope_tables(seq):
    pos = jnp.arange(seq, dtype=jnp.float32)
    inv = jnp.power(ROPE_THETA, -jnp.arange(0, ROT_DIM, 2, dtype=jnp.float32) / ROT_DIM)
    ang = pos[:, None] * inv[None, :]
    return jnp.cos(ang), jnp.sin(ang)

def partial_rope(t, cos, sin):
    tf = t.astype(jnp.float32)
    half = ROT_DIM // 2
    x1, x2, rest = tf[..., :half], tf[..., half:ROT_DIM], tf[..., ROT_DIM:]
    c, s = cos[None, :, None, :], sin[None, :, None, :]
    out = jnp.concatenate([x1 * c - x2 * s, x2 * c + x1 * s, rest], axis=-1)
    return out.astype(t.dtype)

def band_attention(q, k, v, sink):
    b, s = q.shape[0], q.shape[1]
    nb = s // BLOCK
    qb = q.reshape(b, nb, BLOCK, N_KV_HEADS, GROUP, HEAD_DIM).transpose(1, 0, 2, 3, 4, 5)

    def windows(t):
        tp = jnp.pad(t, ((0, 0), (BLOCK, BLOCK), (0, 0), (0, 0)))
        tb = tp.reshape(b, nb + 2, BLOCK, N_KV_HEADS, HEAD_DIM)
        w = jnp.concatenate([tb[:, :-2], tb[:, 1:-1], tb[:, 2:]], axis=2)
        return w.transpose(1, 0, 2, 3, 4)

    kw, vw = windows(k), windows(v)
    blk = jnp.arange(nb)
    q_idx = blk[:, None] * BLOCK + jnp.arange(BLOCK)[None, :]
    k_idx = (blk[:, None] - 1) * BLOCK + jnp.arange(3 * BLOCK)[None, :]
    mask = ((jnp.abs(q_idx[:, :, None] - k_idx[:, None, :]) <= WINDOW)
            & (k_idx[:, None, :] >= 0) & (k_idx[:, None, :] < s))
    sink_f = sink.astype(jnp.float32).reshape(N_KV_HEADS, GROUP)[None, :, :, None, None]
    scale = HEAD_DIM ** -0.5

    def one_block(args):
        qi, ki, vi, mi = args
        sc = jnp.einsum('bqkgd,bskd->bkgqs', qi.astype(jnp.float32), ki.astype(jnp.float32)) * scale
        sc = jnp.where(mi[None, None, None], sc, NEG_INF)
        m = jnp.maximum(jnp.max(sc, axis=-1, keepdims=True), sink_f)
        p = jnp.exp(sc - m)
        denom = jnp.sum(p, axis=-1, keepdims=True) + jnp.exp(sink_f - m)
        o = jnp.einsum('bkgqs,bskd->bqkgd', p / denom, vi.astype(jnp.float32))
        return o.astype(qi.dtype)

    o = lax.map(one_block, (qb, kw, vw, mask))
    return o.transpose(1, 0, 2, 3, 4, 5).reshape(b, s, Q_W)

def short_conv(u, w):
    up = jnp.pad(u, ((0, 0), (1, 1), (0, 0)))
    return up[:, :-2] * w[0] + up[:, 1:-1] * w[1] + up[:, 2:] * w[2]

def first_inputs(seed: int = 0) -> dict:
    key = jax.random.key(seed)
    ks = jax.random.split(key, 16)
    f32 = jnp.float32

    def nrm(k, shape, fan_in):
        return jax.random.normal(k, shape, f32) * (fan_in ** -0.5)

    def gain(k):
        return 1.0 + 0.05 * jax.random.normal(k, (DEPTH, D_MODEL), f32)

    return {
        "x": jax.random.normal(ks[0], (BATCH, SEQ, D_MODEL), f32),
        "g_pre_mix": gain(ks[1]),
        "w_in": nrm(ks[2], (DEPTH, D_MODEL, IN_COLS), D_MODEL),
        "attn_sink": 0.5 * jax.random.normal(ks[3], (DEPTH, N_HEADS), f32),
        "conv_w": nrm(ks[4], (DEPTH, CONV_K, CONV_WIDTH), CONV_K),
        "w_attn_proj": nrm(ks[5], (DEPTH, Q_W, D_MODEL), Q_W),
        "w_conv_proj": nrm(ks[6], (DEPTH, CONV_WIDTH, D_MODEL), CONV_WIDTH),
        "w_out": nrm(ks[7], (DEPTH, D_MODEL, D_MODEL), D_MODEL),
        "g_post_mix": gain(ks[8]),
        "g_pre_ffn": gain(ks[9]),
        "w_gate": nrm(ks[10], (DEPTH, D_MODEL, D_FF), D_MODEL),
        "w_up": nrm(ks[11], (DEPTH, D_MODEL, D_FF), D_MODEL),
        "w_down": nrm(ks[12], (DEPTH, D_FF, D_MODEL), D_FF),
        "g_post_ffn": gain(ks[13]),
    }

def first_block(x, g_pre_mix, w_in, attn_sink, conv_w, w_attn_proj, w_conv_proj, w_out,
              g_post_mix, g_pre_ffn, w_gate, w_up, w_down, g_post_ffn):
    b, s, _ = x.shape
    cos, sin = rope_tables(s)
    splits = np.cumsum([Q_W, KV_W, KV_W, CONV_WIDTH, CONV_WIDTH, CONV_WIDTH, D_MODEL]).tolist()
    for l in range(DEPTH):
        h = rms_norm(x, g_pre_mix[l])
        z = h @ w_in[l]
        q, k, v, cb, cc, cx, ga, gb = jnp.split(z, splits, axis=-1)
        q = partial_rope(q.reshape(b, s, N_HEADS, HEAD_DIM), cos, sin)
        k = partial_rope(k.reshape(b, s, N_KV_HEADS, HEAD_DIM), cos, sin)
        v = v.reshape(b, s, N_KV_HEADS, HEAD_DIM)
        y_attn = band_attention(q, k, v, attn_sink[l]) @ w_attn_proj[l]
        y_conv = (cb * short_conv(cc * cx, conv_w[l])) @ w_conv_proj[l]
        mix = (jax.nn.sigmoid(ga) * y_attn + jax.nn.sigmoid(gb) * y_conv) @ w_out[l]
        x = x + rms_norm(mix, g_post_mix[l])
        h = rms_norm(x, g_pre_ffn[l])
        f = (jax.nn.silu(h @ w_gate[l]) * (h @ w_up[l])) @ w_down[l]
        x = x + rms_norm(f, g_post_ffn[l])
    return x


CHUNK = 64
N_A_LAYERS = DEPTH // 2
N_B_LAYERS = DEPTH - N_A_LAYERS
EPS = 1e-6

MA_HEADS = 8
MA_QK = 64
MA_V = D_MODEL // MA_HEADS
MA_CONV = 4
MA_QK_COLS = 2 * MA_HEADS * MA_QK
MA_PROJ = MA_QK_COLS + 2 * D_MODEL + 2 * MA_HEADS

SB_HEADS = 16
SB_DIM = D_MODEL // SB_HEADS
SB_BLOCK = 128

PEER_HEADS = 8
PEER_NKEYS = 128
PEER_EXPERTS = PEER_NKEYS * PEER_NKEYS
PEER_QDIM = 256
PEER_TOPK = 16
PEER_BLOCK = 128


def rmsnorm(x, g):
    xf = x.astype(jnp.float32)
    y = xf * lax.rsqrt(jnp.mean(xf * xf, axis=-1, keepdims=True) + EPS)
    return (y * g.astype(jnp.float32)).astype(x.dtype)

def ada_mod(c, w, b):
    return jnp.einsum('bd,de->be', jax.nn.silu(c), w) + b

def modulate(h, shift, scale):
    return h * (1.0 + scale[:, None, :]) + shift[:, None, :]

def causal_conv(x, w):
    width, ch = w.shape
    return lax.conv_general_dilated(x, w[:, None, :], window_strides=(1,), padding=[(width - 1, 0)],
                                    dimension_numbers=('NWC', 'WIO', 'NWC'), feature_group_count=ch)

def mlstm_mixer(h, w_in, conv_w, b_if, hnorm_g, w_out):
    bsz, seq, _ = h.shape
    nc = seq // CHUNK
    proj = jnp.einsum('bsd,de->bse', h, w_in)
    qk, v, o, gates = jnp.split(proj, [MA_QK_COLS, MA_QK_COLS + D_MODEL, MA_QK_COLS + 2 * D_MODEL], axis=-1)
    qk = jax.nn.silu(causal_conv(qk, conv_w))
    q, k = jnp.split(qk, 2, axis=-1)
    gates = (gates + b_if).astype(jnp.float32)
    i_pre, f_pre = jnp.split(gates, 2, axis=-1)

    def to_chunks(t, d):
        return t.reshape(bsz, nc, CHUNK, MA_HEADS, d).transpose(0, 3, 1, 2, 4)

    q = to_chunks(q, MA_QK).astype(jnp.float32) * (MA_QK ** -0.5)
    k = to_chunks(k, MA_QK).astype(jnp.float32)
    v = to_chunks(v, MA_V).astype(jnp.float32)
    i_pre = i_pre.reshape(bsz, nc, CHUNK, MA_HEADS).transpose(0, 3, 1, 2)
    log_f = jax.nn.log_sigmoid(f_pre).reshape(bsz, nc, CHUNK, MA_HEADS).transpose(0, 3, 1, 2)
    b = jnp.cumsum(log_f, axis=-1)
    b_last = b[..., -1]

    w_state = b_last[..., None] - b + i_pre
    m_loc = jnp.max(w_state, axis=-1)
    e_state = jnp.exp(w_state - m_loc[..., None])
    c_loc = jnp.einsum('bhcl,bhclv,bhclk->bhcvk', e_state, v, k)
    n_loc = jnp.einsum('bhcl,bhclk->bhck', e_state, k)

    def step(carry, inp):
        c_st, n_st, m_st = carry
        cl, nl, ml, bl = inp
        m_new = jnp.maximum(bl + m_st, ml)
        a = jnp.exp(bl + m_st - m_new)
        r = jnp.exp(ml - m_new)
        c_new = a[..., None, None] * c_st + r[..., None, None] * cl
        n_new = a[..., None] * n_st + r[..., None] * nl
        return (c_new, n_new, m_new), (c_st, n_st, m_st)

    init = (jnp.zeros((bsz, MA_HEADS, MA_V, MA_QK), jnp.float32),
            jnp.zeros((bsz, MA_HEADS, MA_QK), jnp.float32),
            jnp.zeros((bsz, MA_HEADS), jnp.float32))
    xs = (c_loc.transpose(2, 0, 1, 3, 4), n_loc.transpose(2, 0, 1, 3),
          m_loc.transpose(2, 0, 1), b_last.transpose(2, 0, 1))
    _, (c_prev, n_prev, m_prev) = lax.scan(step, init, xs)
    c_prev = c_prev.transpose(1, 2, 0, 3, 4)
    n_prev = n_prev.transpose(1, 2, 0, 3)
    m_prev = m_prev.transpose(1, 2, 0)

    causal = jnp.tril(jnp.ones((CHUNK, CHUNK), dtype=bool))
    log_d = jnp.where(causal, b[..., :, None] - b[..., None, :] + i_pre[..., None, :], -jnp.inf)
    inter_log = b + m_prev[..., None]
    m_t = jnp.maximum(inter_log, jnp.max(log_d, axis=-1))
    inter_w = jnp.exp(inter_log - m_t)
    s_qk = jnp.einsum('bhcld,bhcsd->bhcls', q, k) * jnp.exp(log_d - m_t[..., None])
    num = jnp.einsum('bhcls,bhcsv->bhclv', s_qk, v) + inter_w[..., None] * jnp.einsum('bhcvk,bhclk->bhclv', c_prev, q)
    den = jnp.sum(s_qk, axis=-1) + inter_w * jnp.einsum('bhck,bhclk->bhcl', n_prev, q)
    hh = num / jnp.maximum(jnp.abs(den), jnp.exp(-m_t))[..., None]
    hh = hh.transpose(0, 2, 3, 1, 4).reshape(bsz, seq, MA_HEADS, MA_V)
    hh = rmsnorm(hh, hnorm_g) * jax.nn.sigmoid(o.astype(jnp.float32)).reshape(bsz, seq, MA_HEADS, MA_V)
    return jnp.einsum('bse,ed->bsd', hh.reshape(bsz, seq, D_MODEL).astype(h.dtype), w_out)

def shared_kv(x, c, kv_ada_w, kv_ada_b, kv_norm_g, kv_w, k_norm_g):
    bsz, seq, _ = x.shape
    shift, scale = jnp.split(ada_mod(c, kv_ada_w, kv_ada_b), 2, axis=-1)
    h = modulate(rmsnorm(x, kv_norm_g), shift, scale)
    kv = jnp.einsum('bsd,de->bse', h, kv_w)
    k, v = jnp.split(kv, 2, axis=-1)
    k = rmsnorm(k.reshape(bsz, seq, SB_HEADS, SB_DIM), k_norm_g).transpose(0, 2, 1, 3)
    v = v.reshape(bsz, seq, SB_HEADS, SB_DIM).transpose(0, 2, 1, 3)
    return k, v

def stick_breaking_mixer(h, k, v, w_q, q_norm_g, w_out):
    bsz, seq, _ = h.shape
    q = jnp.einsum('bsd,de->bse', h, w_q).reshape(bsz, seq, SB_HEADS, SB_DIM)
    q = (rmsnorm(q, q_norm_g) * (SB_DIM ** -0.5)).transpose(0, 2, 1, 3)
    outs = []
    for blk in range(seq // SB_BLOCK):
        t0 = blk * SB_BLOCK
        end = t0 + SB_BLOCK
        z = jnp.einsum('bhtd,bhsd->bhts', q[:, :, t0:end], k[:, :, :end]).astype(jnp.float32)
        strict = jnp.arange(end)[None, :] < (t0 + jnp.arange(SB_BLOCK))[:, None]
        log1m = jnp.where(strict, -jax.nn.softplus(z), 0.0)
        between = lax.cumsum(log1m, axis=3, reverse=True) - log1m
        a = jnp.where(strict, jnp.exp(jax.nn.log_sigmoid(z) + between), 0.0)
        outs.append(jnp.einsum('bhts,bhsd->bhtd', a, v[:, :, :end].astype(jnp.float32)))
    o = jnp.concatenate(outs, axis=2).transpose(0, 2, 1, 3).reshape(bsz, seq, D_MODEL)
    return jnp.einsum('bse,ed->bsd', o.astype(h.dtype), w_out)

def peer_ffn(h, w_q, sub_keys, peer_u, peer_v):
    bsz, seq, d = h.shape
    xt = h.reshape(bsz * seq // PEER_BLOCK, PEER_BLOCK, d)

    def block(xb):
        q = jnp.einsum('td,de->te', xb, w_q).reshape(PEER_BLOCK, PEER_HEADS, 2, PEER_QDIM // 2)
        s = jnp.einsum('thpk,pnk->thpn', q, sub_keys).astype(jnp.float32)
        s_top, i_top = lax.top_k(s, PEER_TOPK)
        cand = (s_top[:, :, 0, :, None] + s_top[:, :, 1, None, :]).reshape(PEER_BLOCK, PEER_HEADS, PEER_TOPK * PEER_TOPK)
        cand_idx = (i_top[:, :, 0, :, None] * PEER_NKEYS + i_top[:, :, 1, None, :]).reshape(PEER_BLOCK, PEER_HEADS, PEER_TOPK * PEER_TOPK)
        g_top, pos = lax.top_k(cand, PEER_TOPK)
        expert = jnp.take_along_axis(cand_idx, pos, axis=-1)
        g = jax.nn.softmax(g_top, axis=-1)
        u = jnp.take(peer_u, expert, axis=0)
        act = jax.nn.gelu(jnp.einsum('thkd,td->thk', u, xb).astype(jnp.float32), approximate=False)
        vv = jnp.take(peer_v, expert, axis=0)
        return jnp.einsum('thk,thkd->td', (g * act).astype(xb.dtype), vv)

    return lax.map(block, xt).reshape(bsz, seq, d)

def second_inputs(seed: int = 0) -> dict:
    key = jax.random.key(seed)
    ks = jax.random.split(key, 24)
    f32 = jnp.float32
    d = D_MODEL

    def nrm(k, shape, scale):
        return jax.random.normal(k, shape, f32) * scale

    def gain(k, shape):
        return 1.0 + 0.02 * jax.random.normal(k, shape, f32)

    if_base = jnp.concatenate([jnp.zeros((MA_HEADS,), f32), jnp.linspace(3.0, 6.0, MA_HEADS, dtype=f32)])
    return {
        'x': nrm(ks[0], (BATCH, SEQ, d), 1.0),
        'c': nrm(ks[1], (BATCH, d), 1.0),
        'ada_w': nrm(ks[2], (DEPTH, d, 6 * d), 0.5 * d ** -0.5),
        'ada_b': nrm(ks[3], (DEPTH, 6 * d), 0.01),
        'norm_mix_g': gain(ks[4], (DEPTH, d)),
        'norm_ffn_g': gain(ks[5], (DEPTH, d)),
        'ma_w_in': nrm(ks[6], (N_A_LAYERS, d, MA_PROJ), d ** -0.5),
        'ma_conv_w': nrm(ks[7], (N_A_LAYERS, MA_CONV, MA_QK_COLS), MA_CONV ** -0.5),
        'ma_b_if': if_base + nrm(ks[8], (N_A_LAYERS, 2 * MA_HEADS), 0.1),
        'ma_hnorm_g': gain(ks[9], (N_A_LAYERS, MA_HEADS, MA_V)),
        'ma_w_out': nrm(ks[10], (N_A_LAYERS, d, d), d ** -0.5),
        'kv_ada_w': nrm(ks[11], (d, 2 * d), 0.5 * d ** -0.5),
        'kv_ada_b': nrm(ks[12], (2 * d,), 0.01),
        'kv_norm_g': gain(ks[13], (d,)),
        'kv_w': nrm(ks[14], (d, 2 * d), d ** -0.5),
        'k_norm_g': gain(ks[15], (SB_DIM,)),
        'sb_w_q': nrm(ks[16], (N_B_LAYERS, d, d), d ** -0.5),
        'sb_q_norm_g': gain(ks[17], (N_B_LAYERS, SB_DIM)),
        'sb_w_out': nrm(ks[18], (N_B_LAYERS, d, d), d ** -0.5),
        'peer_w_q': nrm(ks[19], (DEPTH, d, PEER_HEADS * PEER_QDIM), d ** -0.5),
        'peer_sub_keys': nrm(ks[20], (DEPTH, 2, PEER_NKEYS, PEER_QDIM // 2), (PEER_QDIM // 2) ** -0.5),
        'peer_u': nrm(ks[21], (DEPTH, PEER_EXPERTS, d), d ** -0.5),
        'peer_v': nrm(ks[22], (DEPTH, PEER_EXPERTS, d), PEER_HEADS ** -0.5),
    }

def second_block(x, c, ada_w, ada_b, norm_mix_g, norm_ffn_g, ma_w_in, ma_conv_w, ma_b_if, ma_hnorm_g, ma_w_out,
              kv_ada_w, kv_ada_b, kv_norm_g, kv_w, k_norm_g, sb_w_q, sb_q_norm_g, sb_w_out,
              peer_w_q, peer_sub_keys, peer_u, peer_v):
    k_sh = None
    v_sh = None
    for layer in range(DEPTH):
        sh1, sc1, g1, sh2, sc2, g2 = jnp.split(ada_mod(c, ada_w[layer], ada_b[layer]), 6, axis=-1)
        h = modulate(rmsnorm(x, norm_mix_g[layer]), sh1, sc1)
        if layer < N_A_LAYERS:
            y = mlstm_mixer(h, ma_w_in[layer], ma_conv_w[layer], ma_b_if[layer], ma_hnorm_g[layer], ma_w_out[layer])
        else:
            if layer == N_A_LAYERS:
                k_sh, v_sh = shared_kv(x, c, kv_ada_w, kv_ada_b, kv_norm_g, kv_w, k_norm_g)
            j = layer - N_A_LAYERS
            y = stick_breaking_mixer(h, k_sh, v_sh, sb_w_q[j], sb_q_norm_g[j], sb_w_out[j])
        x = x + g1[:, None, :] * y
        h = modulate(rmsnorm(x, norm_ffn_g[layer]), sh2, sc2)
        x = x + g2[:, None, :] * peer_ffn(h, peer_w_q[layer], peer_sub_keys[layer], peer_u[layer], peer_v[layer])
    return x


def setup_inputs(seed=0):
    out = dict(first_inputs(seed))
    for name, value in second_inputs(seed + 1).items():
        if name != "x":
            out[name + "_2"] = value
    return out


def reference(
    x, g_pre_mix, w_in, attn_sink, conv_w, w_attn_proj, w_conv_proj, w_out, g_post_mix,
    g_pre_ffn, w_gate, w_up, w_down, g_post_ffn, c_2, ada_w_2, ada_b_2, norm_mix_g_2,
    norm_ffn_g_2, ma_w_in_2, ma_conv_w_2, ma_b_if_2, ma_hnorm_g_2, ma_w_out_2, kv_ada_w_2,
    kv_ada_b_2, kv_norm_g_2, kv_w_2, k_norm_g_2, sb_w_q_2, sb_q_norm_g_2, sb_w_out_2,
    peer_w_q_2, peer_sub_keys_2, peer_u_2, peer_v_2,
):
    x = first_block(
        x, g_pre_mix, w_in, attn_sink, conv_w, w_attn_proj, w_conv_proj, w_out, g_post_mix,
        g_pre_ffn, w_gate, w_up, w_down, g_post_ffn,
    )
    return second_block(
        x, c_2, ada_w_2, ada_b_2, norm_mix_g_2, norm_ffn_g_2, ma_w_in_2, ma_conv_w_2, ma_b_if_2,
        ma_hnorm_g_2, ma_w_out_2, kv_ada_w_2, kv_ada_b_2, kv_norm_g_2, kv_w_2, k_norm_g_2,
        sb_w_q_2, sb_q_norm_g_2, sb_w_out_2, peer_w_q_2, peer_sub_keys_2, peer_u_2, peer_v_2,
    )


_drawn_inputs = setup_inputs


def setup_inputs(seed=0):
    import zlib

    import numpy as np

    out = dict(_drawn_inputs(seed))
    spreads = {}
    factors = {'attn_sink': 8.0,
     'ada_b_2': 8.0,
     'norm_mix_g_2': 8.0,
     'norm_ffn_g_2': 8.0,
     'ma_hnorm_g_2': 8.0,
     'kv_ada_b_2': 8.0,
     'kv_norm_g_2': 8.0,
     'k_norm_g_2': 8.0,
     'sb_q_norm_g_2': 8.0}
    for name, (base, spread) in spreads.items():
        noise = np.random.default_rng([zlib.crc32(name.encode()), seed]).standard_normal(out[name].shape)
        drawn = base * np.exp(spread * noise) if base else spread * noise
        out[name] = __import__('jax').numpy.asarray(drawn.astype(out[name].dtype))
    for name, factor in factors.items():
        out[name] = (out[name] * factor).astype(out[name].dtype)
    return out
```

```python
import math
from contextlib import ExitStack

import numpy as np

import concourse.bass as bass
from concourse import mybir

F32 = mybir.dt.float32
I32 = mybir.dt.int32
U32 = mybir.dt.uint32
ALU = mybir.AluOpType
ACT = mybir.ActivationFunctionType
AX = mybir.AxisListType

P = 128
D = 1024
SEQ = 256
NT = SEQ // P
KC = D // P
DEPTH = 2
HEADS, KV_HEADS, HD = 16, 4, 64
GROUP = HEADS // KV_HEADS
ROT = HD // 4
HALF = ROT // 2
THETA = 500000.0
WINDOW = 128
D_FF = 2816
FC = D_FF // P
EPS = 1e-6
NEG = -1e30

R = 4
COLS = 512
SLOTS_A = 36
Q_S, KV_S, CB_S, CC_S, CX_S, GA_S, GB_S = 0, 2, 3, 5, 7, 9, 11
CONVP_S, ATTNP_S, OUT_S, FFN_S, DOWN_S = 13, 15, 17, 19, 30
Q0, KV0, CB0, CC0, CX0, GA0, GB0 = 0, 1024, 1536, 2560, 3584, 4608, 5632
DOWN_PIECES = [(0, 8), (8, 8), (16, 6)]

D_UNITS = 4 + 4 + 4 + 4 + 4 + FC
A_UNITS = 4 + 2 + 4 + 6 + 4 + 4 + 4 + 4
G_PRE, G_FFN, CONVW = 0, KC, 2 * KC
NCOL = 2 * KC + 3 * KC

LSTM_HEADS, LSTM_QK, LSTM_V, LSTM_CONV = 8, 64, 128, 4
SB_HEADS, SB_DIM = 16, 64
PEER_HEADS, NKEYS, TOPK = 8, 128, 16
EXPERTS = NKEYS * NKEYS
ADA_CHUNKS = 2 * 6 * KC + 2 * KC
ADA_LAYER = ADA_CHUNKS // DEPTH
KV_ADA = 2 * 6 * KC
PICKS = PEER_HEADS * TOPK
RING = 8
PAIR = 2 * TOPK
TURNS = PICKS // PAIR
S2 = DEPTH * SLOTS_A
N_MIX, N_FFN, N_KV, LCONV = 0, 2 * KC, 4 * KC, 5 * KC
NCOL2 = 5 * KC + LSTM_CONV * KC
PEER_A_UNITS = 4 + 8 + 8
LSTM_A_UNITS = 8 + 8 + LSTM_HEADS + 4
STICK_FULL = DEPTH * A_UNITS + LSTM_A_UNITS + PEER_A_UNITS + 12 + 8 + 2


def build(nc, ins, out):
    ctx = ExitStack()
    with ctx:
        def sem(name):
            return ctx.enter_context(nc.semaphore(name))

        def psum(name):
            return ctx.enter_context(nc.psum_tensor(name, [P, 512], F32))

        def sb(name, shape, dt=F32, stack=ctx):
            return stack.enter_context(nc.sbuf_tensor(name, shape, dt))

        ident = sb("ident", [P, P])
        x = sb("x", [P, NT, D])
        xn = sb("xn", [P, NT, D])
        hT = sb("hT", [P, KC, SEQ])
        wring = sb("wring", [P, R, KC, COLS])
        adac = sb("adac", [P, ADA_CHUNKS])
        adal = sb("adal", [P, ADA_LAYER])
        cols2 = sb("cols2", [P, NCOL2])
        adab = sb("adab", [P, ADA_CHUNKS])
        rsb = sb("rsb", [P, 32])
        modA = sb("modA", [P, 5, KC])
        cols = sb("cols", [P, NCOL])
        ssx = sb("ssx", [P, NT])
        rsx = sb("rsx", [P, NT])
        ssm = sb("ssm", [P, NT, 2])
        rsm = sb("rsm", [P, NT])
        junk = sb("junk", [P, D])
        rsv, rsa = sb("rsv", [P, 32]), sb("rsa", [P, 32])

        first = ExitStack()
        def sa(name, shape, dt=F32):
            return sb(name, shape, dt, first)
        rows = sa("rows", [P, 2, D])
        crow = sa("crow", [P, D])
        aring = sa("aring", [P, 2, D])
        mask8 = sa("mask8", [P, NT, SEQ])
        cs = sa("cs", [P, 2, NT, HALF])
        sinks = sa("sinks", [P, HEADS])
        cbT = sa("cbT", [P, KC, SEQ])
        ccT = sa("ccT", [P, KC, SEQ])
        uT = sa("uT", [P, KC, SEQ + 2])
        cvt = sa("cvt", [P, 2, SEQ])
        sga = sa("sga", [P, KC, SEQ])
        sgb = sa("sgb", [P, KC, SEQ])
        silu = sa("silu", [P, 2, SEQ])
        att = ExitStack()
        def st(name, shape, dt=F32):
            return sb(name, shape, dt, att)
        zrow = st("zrow", [P, NT, Q0 + CB0])
        kdup = st("kdup", [P, NT, KV_HEADS, 2, HD])
        qT = st("qT", [P, KC, SEQ])
        kT = st("kT", [P, KV_HEADS, SEQ])
        rt = st("rt", [P, 4, NT * (HEADS + KV_HEADS) * HALF])
        S = st("S", [P, 2, NT, SEQ])
        PR = st("PR", [P, 2, NT, SEQ])
        PT = st("PT", [P, 2, NT, SEQ])
        nm = st("nm", [P, HEADS, NT])
        rmx = st("rmx", [P, HEADS, NT])
        den = st("den", [P, HEADS, NT])
        es = st("es", [P, 4, NT])
        rden = st("rden", [P, NT, 4])
        att.close()
        fT = sa("fT", [P, FC, SEQ])
        orow = xn
        oT = qT
        first.close()

        grows = sb("grows", [P, 4, D])
        lstm = ExitStack()
        def sl(name, shape, dt=F32):
            return sb(name, shape, dt, lstm)
        biglm = sl("biglm", [P, 3 * P])
        wg = sl("wg", [P, KC, 2 * LSTM_HEADS])
        bif = sl("bif", [LSTM_HEADS, 2])
        hng = sl("hng", [P, D])
        preT = sl("preT", [P, KC, SEQ + LSTM_CONV - 1])
        lcv = sl("lcv", [P, 2, SEQ])
        qkT = sl("qkT", [P, KC, SEQ])
        vaug = sl("vaug", [P, NT, LSTM_HEADS, LSTM_V + 1])
        so = sl("so", [P, NT, D])
        numS = sl("numS", [P, LSTM_HEADS, NT, LSTM_V + 1])
        gi, gf, ge, gl, gb_, gg, gM, gm, gone = [sl(n, [LSTM_HEADS, SEQ]) for n in
                                                 ("gi", "gf", "ge", "gl", "gb_", "gg", "gM", "gm", "gone")]
        gcol = sl("gcol", [P, 4, LSTM_HEADS])
        Dt = sl("Dt", [P, 2, 3 * P])
        Pl = sl("Pl", [P, 2, 3 * P])
        dcol = sl("dcol", [P, LSTM_HEADS, NT])
        rcol = sl("rcol", [P, LSTM_HEADS * NT])
        lstm.close()

        stick = ExitStack()
        def sk(name, shape, dt=F32):
            return sb(name, shape, dt, stick)
        strict = sk("strict", [P, 3 * P])
        tri = sk("tri", [P, P])
        ones = sk("ones", [P, P])
        qkg = sk("qkg", [P, 2, SB_DIM])
        hkT = sk("hkT", [P, KC, SEQ])
        srow = sk("srow", [P, 3, NT, D])
        skT = sk("skT", [P, KC, SEQ])
        sqT = sk("sqT", [P, KC, SEQ])
        sqs = sk("sqs", [P, NT, D])
        srs, sss = sk("srs", [P, NT * SB_HEADS]), sk("sss", [P, NT * SB_HEADS])
        az, sL, sp_, ls, ex = [sk(n, [P, 2, 3 * P]) for n in ("az", "sL", "sp_", "ls", "ex")]
        stick.close()

        experts = ExitStack()
        def se(name, shape, dt=F32):
            return sb(name, shape, dt, experts)
        keysT = se("keysT", [P, 2, NKEYS])
        iota = se("iota", [P, TOPK])
        gring = se("gring", [P, RING, D])
        hrow = se("hrow", [P, NT, D])
        qpT = se("qpT", [P, 2 * PEER_HEADS, SEQ])
        sc = se("sc", [P, NT, 2 * PEER_HEADS, NKEYS])
        sc2 = se("sc2", [P, 2 * PEER_HEADS, NKEYS])
        top = se("top", [P, PEER_HEADS, 2, TOPK])
        topi = se("topi", [P, PEER_HEADS, 2, TOPK], U32)
        topf = se("topf", [P, PEER_HEADS, 2, TOPK])
        gt = se("gt", [P, PEER_HEADS, TOPK])
        pos = se("pos", [P, PEER_HEADS, TOPK], U32)
        hilo = se("hilo", [P, 2, PICKS], U32)
        hilof = se("hilof", [P, 2, PICKS])
        ef = se("ef", [P, 2, PICKS])
        eidx = se("eidx", [P, NT, PICKS + PAIR], I32)
        wsum = se("wsum", [P, PEER_HEADS])
        wexp = se("wexp", [P, NT, PEER_HEADS, TOPK])
        ix = se("ix", [P, 2, TOPK], I32)
        a16 = se("a16", [P, 2, TOPK])
        dots = se("dots", [P, PICKS])
        coef = se("coef", [P, PICKS])
        acc = junk
        cand = qpT[:, 0:PEER_HEADS, :]
        pick = qpT[:, PEER_HEADS:2 * PEER_HEADS, :]
        experts.close()

        pd = [psum("pd0"), psum("pd1")]
        pa = [psum("pa0"), psum("pa1")]
        pr = [psum(f"pr{i}") for i in range(4)]
        psc, ppt, po = pr[0:2], pr[2], pr[3]

        w_in_slot = [sem(f"w_in_slot{i}") for i in range(R)]
        w_free = sem("w_free")
        x_in = sem("x_in")
        const_in = sem("const_in")
        par_in = sem("par_in")
        par_free = sem("par_free")
        pd_full, pd_free = sem("pd_full"), sem("pd_free")
        pa_full, pa_free = sem("pa_full"), sem("pa_free")
        x_ready = sem("x_ready")
        ss_ready = sem("ss_ready")
        xn_ready = sem("xn_ready")
        hT_ready = sem("hT_ready")
        rope_done = sem("rope_done")
        qk_ready = sem("qk_ready")
        sc_full, sc_seen, sc_read = sem("sc_full"), sem("sc_seen"), sem("sc_read")
        nm_ready, p_ready = sem("nm_ready"), sem("p_ready")
        pt_full, pt_ready = sem("pt_full"), sem("pt_ready")
        o_full, o_read = sem("o_full"), sem("o_read")
        o_used = sem("o_used")
        o_rows = sem("o_rows")
        es_sum, es_ready = sem("es_sum"), sem("es_ready")
        cc_ready = sem("cc_ready")
        sig_ready = sem("sig_ready")
        yconv_ready = sem("yconv_ready")
        mix_ready = sem("mix_ready")
        row_full, row_read = sem("row_full"), sem("row_read")
        ssm_ready = sem("ssm_ready")
        silu_ready, silu_free = sem("silu_ready"), sem("silu_free")
        f_ready = sem("f_ready")
        out_done = sem("out_done")
        c_in, c_ready = sem("c_in"), sem("c_ready")
        ada_in, ada_free, ada_ready = [sem("ada_in0"), sem("ada_in1")], sem("ada_free"), sem("ada_ready")
        cols2_in, lstm_in, stick_in, experts_in = sem("cols2_in"), sem("lstm_in"), sem("stick_in"), sem("experts_in")
        mod_ready = sem("mod_ready")
        grows_ready = sem("grows_ready")
        v_ready = sem("v_ready")
        qk_pre, qk_silu = sem("qk_pre"), sem("qk_silu")
        if_full, if_abs, if_log, if_sum, if_exp = sem("if_full"), sem("if_abs"), sem("if_log"), sem("if_sum"), sem("if_exp")
        gcol_full, gcol_ready = sem("gcol_full"), sem("gcol_ready")
        m_full, m_read, st_full, st_read = sem("m_full"), sem("m_read"), sem("st_full"), sem("st_read")
        d_pre, d_ready, pl_ready = sem("d_pre"), sem("d_ready"), sem("pl_ready")
        num_ready, y_rows = sem("num_ready"), sem("y_rows")
        yT_ready = sem("yT_ready")
        srow_ready, sqk_ready, sT_ready = sem("srow_ready"), sem("sqk_ready"), sem("sT_ready")
        z_full, z_read, sL_ready = sem("z_full"), sem("z_read"), sem("sL_ready")
        spm_ready, cum_full, cum_read = sem("spm_ready"), sem("cum_full"), sem("cum_read")
        sp_ready, ex_ready, a_exp, a_ready, a_used = sem("sp_ready"), sem("ex_ready"), sem("a_exp"), sem("a_ready"), sem("a_used")
        hrow_ready, qp_ready, sc_ready = sem("hrow_ready"), sem("qp_ready"), sem("sc_ready")
        g_arg, g_exp = sem("g_arg"), sem("g_exp")
        ix_ready, rows_free, wait_seen = sem("ix_ready"), sem("rows_free"), sem("wait_seen")
        row_in = [sem(f"row_in{i}") for i in range(RING)]
        dots_ready, gelu_ready = sem("dots_ready"), sem("gelu_ready")

        wcol = {k: ins[k] for k in ("w_in", "w_attn_proj", "w_conv_proj", "w_out", "w_gate", "w_up", "w_down")}

        block = ctx.enter_context(nc.Block())

        def slot(i):
            return wring[:, i % R]

        @block.sync
        def _(sp):
            sp.dma_start(crow[:, :], ins["c_2"].partition_broadcast(P).rearrange("p a n -> p (a n)")).then_inc(c_in, 16)
            sp.dma_start(x[:, :, :], ins["x"].rearrange("b (t p) d -> p (b t) d", p=P)).then_inc(x_in, 16)
            sp.dma_start(ident[:, :], ins["c_ident"]).then_inc(const_in, 16)
            sp.dma_start(mask8[:, :, :], ins["c_mask8"]).then_inc(const_in, 16)
            sp.dma_start(cs[:, :, :, :], ins["c_cs"]).then_inc(const_in, 16)

            def load(l, i, parts):
                sp.wait_ge(w_free, l * SLOTS_A + i + 1)
                for dst, src in parts:
                    sp.dma_start(dst, src).then_inc(w_in_slot[i % R], 16)

            def cut(w, l, c0, n, k0=0, k=KC):
                v = w[bass.ds(l, 1), k0 * P:(k0 + k) * P, c0:c0 + n]
                return v.rearrange("a (k p) n -> p (a k) n", p=P)

            def params(l):
                sp.wait_ge(par_free, 2 * l + 2)
                sp.dma_start(cols[:, :], ins["cols_a"][bass.ds(l, 1)].rearrange("a p n -> p (a n)")).then_inc(par_in, 16)
                sp.dma_start(sinks[:, :], ins["attn_sink"][bass.ds(l, 1), :].partition_broadcast(P).rearrange("p a h -> p (a h)")).then_inc(par_in, 16)
                sp.dma_start(rows[:, 0, :], ins["g_post_mix"][bass.ds(l, 1), :].partition_broadcast(P).rearrange("p a h -> p (a h)")).then_inc(par_in, 16)
                sp.dma_start(rows[:, 1, :], ins["g_post_ffn"][bass.ds(l, 1), :].partition_broadcast(P).rearrange("p a h -> p (a h)")).then_inc(par_in, 16)

            sp.dma_start(cols2[:, :], ins["cols_b"]).then_inc(cols2_in, 16)
            sp.dma_start(adab[:, :], ins["ada_bias"]).then_inc(cols2_in, 16)
            with sp.Fori(0, DEPTH) as l:
                for i in range(SLOTS_A):
                    if i == 1:
                        params(l)
                    if i < CONVP_S:
                        parts = [(slot(i), cut(ins["w_in"], l, i * COLS, COLS))]
                    elif i < FFN_S:
                        w, s0 = {0: ("w_conv_proj", CONVP_S), 1: ("w_attn_proj", ATTNP_S), 2: ("w_out", OUT_S)}[(i - CONVP_S) // 2]
                        parts = [(slot(i), cut(ins[w], l, (i - s0) * COLS, COLS))]
                    elif i < DOWN_S:
                        c0 = (i - FFN_S) * 256
                        parts = [(slot(i)[:, :, 0:256], cut(ins["w_gate"], l, c0, 256)),
                                 (slot(i)[:, :, 256:512], cut(ins["w_up"], l, c0, 256))]
                    else:
                        h, (k0, k) = (i - DOWN_S) // 3, DOWN_PIECES[(i - DOWN_S) % 3]
                        parts = [(slot(i)[:, 0:k, :], cut(ins["w_down"], l, h * COLS, COLS, k0, k))]
                    load(l, i, parts)
            plan = [("ma_w_in_2", 0, c * COLS) for c in range(6)] + [("ma_w_out_2", 0, c * COLS) for c in range(2)]
            plan += [("peer_w_q_2", 0, c * COLS) for c in range(4)]
            plan += [("kv_w_2", 0, c * COLS) for c in range(4)] + [("sb_w_q_2", 0, c * COLS) for c in range(2)]
            plan += [("sb_w_out_2", 0, c * COLS) for c in range(2)] + [("peer_w_q_2", 1, c * COLS) for c in range(4)]

            def small_lstm():
                sp.wait_ge(x_ready, 2 * DEPTH + 1)
                sp.dma_start(biglm[:, :], ins["c_biglm"]).then_inc(lstm_in, 16)
                sp.dma_start(wg[:, :, :], ins["ma_w_in_2"][0, :, 6 * COLS:6 * COLS + 16].rearrange("(k p) n -> p k n", p=P)).then_inc(lstm_in, 16)
                sp.dma_start(bif[:, :], ins["b_if"]).then_inc(lstm_in, 16)
                sp.dma_start(hng[:, :], ins["hnorm"].partition_broadcast(P).rearrange("p a n -> p (a n)")).then_inc(lstm_in, 16)

            def small_experts(l):
                sp.wait_ge(x_ready, 2 * DEPTH + 2 + 2 * l)
                sp.dma_start(keysT[:, :, :], ins["keysT"][l]).then_inc(experts_in, 16)
                sp.dma_start(iota[:, :], ins["c_iota"]).then_inc(experts_in, 16)

            def small_stick():
                sp.wait_ge(x_ready, 2 * DEPTH + 3)
                sp.dma_start(strict[:, :], ins["c_strict"]).then_inc(stick_in, 16)
                sp.dma_start(tri[:, :], ins["c_tri"]).then_inc(stick_in, 16)
                sp.dma_start(ones[:, :], ins["c_ones"]).then_inc(stick_in, 16)
                sp.dma_start(qkg[:, 0, :], ins["k_norm_g_2"].rearrange("(a n) -> a n", a=1).partition_broadcast(P).rearrange("p a n -> p (a n)")).then_inc(stick_in, 16)
                sp.dma_start(qkg[:, 1, :], ins["sb_q_norm_g_2"].partition_broadcast(P).rearrange("p a n -> p (a n)")).then_inc(stick_in, 16)

            small = {0: small_lstm, 8: lambda: small_experts(0), 12: small_stick, 20: lambda: small_experts(1)}
            for j, (name, l, c0) in enumerate(plan):
                if j - 4 in small:
                    small[j - 4]()
                sp.wait_ge(w_free, S2 + j + 1)
                w = ins[name]
                w = w[l] if len(w.shape) == 3 else w
                sp.dma_start(slot(j), w[:, c0:c0 + COLS].rearrange("(k p) n -> p k n", p=P)).then_inc(w_in_slot[j % R], 16)
            small[20]()
            sp.wait_ge(x_ready, 2 * DEPTH + 5)
            sp.dma_start(out.rearrange("b (t p) d -> p (b t) d", p=P), x[:, :, :]).then_inc(out_done, 16)
            sp.wait_ge(out_done, 16)

        def landed(i):
            n = 0
            for j in range(i + 1):
                if j % R == i % R:
                    n += 32 if FFN_S <= j < DOWN_S else 16
            return n
        LANDED_LAYER = [landed(SLOTS_A - R + r) for r in range(R)]

        @block.tensor
        def _(pe):
            pe.sem_inc(w_free, R)
            pe.wait_ge(const_in, 48)

            def transposes(u, base, src, dst_full):
                ring, full, free = base
                pe.wait_ge(free, u + 1)
                return [nc.tensor.transpose(ring[:, i * P:(i + 1) * P], src(i), ident[:, :]) for i in range(4)][-1].then_inc(full, 1)

            def weights(l, i):
                pe.wait_ge(w_in_slot[i % R], l * LANDED_LAYER[i % R] + landed(i))

            with pe.Fori(0, DEPTH) as l:
                nd, na, owed = [0], [0], [0]

                def used_up():
                    owed[0] += 1

                def mm(out_, lhsT, rhs, start, stop):
                    m = nc.tensor.matmul(out_, lhsT, rhs, start=start, stop=stop)
                    if owed[0] and not stop:
                        m.then_inc(w_free, 1)
                        owed[0] -= 1
                    return m

                def bank_d():
                    u = nd[0]
                    nd[0] += 1
                    pe.wait_ge(pd_free, l * D_UNITS + u + 1)
                    return pd[u % 2]

                def bank_a():
                    u = na[0]
                    na[0] += 1
                    pe.wait_ge(pa_free, l * A_UNITS + u + 1)
                    return pa[u % 2]

                def norm_transposes(n):
                    pe.wait_ge(xn_ready, 2 * l + n + 1)
                    for j in range(KC // 2):
                        b = bank_d()
                        for i in range(4):
                            c, t = 2 * j + i // 2, i % 2
                            m = nc.tensor.transpose(b[:, i * P:(i + 1) * P], xn[:, t, c * P:(c + 1) * P], ident[:, :])
                        m.then_inc(pd_full, 1)

                def row_unit(b, i, t, full, release):
                    for k in range(KC):
                        m = mm(b[:, :], hT[:, k, t * P:(t + 1) * P], slot(i)[:, k, :],
                                             start=(k == 0), stop=(k == KC - 1))
                    m.then_inc(full, 1)
                    if release:
                        used_up()

                def col_unit(b, i, half, src, full, release):
                    for c in range(2):
                        for k in range(KC):
                            m = mm(b[:, c * SEQ:(c + 1) * SEQ], slot(i)[:, k, (2 * half + c) * P:(2 * half + c + 1) * P],
                                                 src[:, k, :], start=(k == 0), stop=(k == KC - 1))
                    m.then_inc(full, 1)
                    if release:
                        used_up()

                norm_transposes(0)
                pe.wait_ge(hT_ready, 2 * l + 1)
                for i in (Q_S, Q_S + 1, KV_S):
                    weights(l, i)
                    for t in range(NT):
                        row_unit(bank_a(), i, t, pa_full, t == 1)
                for i in (CB_S, CB_S + 1):
                    weights(l, i)
                    for half in range(2):
                        col_unit(bank_a(), i, half, hT, pa_full, half == 1)
                pe.wait_ge(rope_done, l + 1)
                for j in range(KC // 2):
                    b = bank_a()
                    for i in range(4):
                        c, t = 2 * j + i // 2, i % 2
                        m = nc.tensor.transpose(b[:, i * P:(i + 1) * P], zrow[:, t, c * P:(c + 1) * P], ident[:, :])
                    m.then_inc(pa_full, 1)
                for j in range(KV_HEADS // 2):
                    b = bank_a()
                    for i in range(4):
                        g, t = 2 * j + i // 2, i % 2
                        m = nc.tensor.transpose(b[:, i * P:(i + 1) * P], kdup[:, t, g].rearrange("p a d -> p (a d)"), ident[:, :])
                    m.then_inc(pa_full, 1)

                def scores(h):
                    if h == 0:
                        pe.wait_ge(qk_ready, l + 1)
                    pe.wait_ge(sc_read, l * HEADS + h + 1)
                    b0 = (h % 2) * HD
                    for t in range(NT):
                        m = mm(psc[h % 2][:, t * SEQ:(t + 1) * SEQ], qT[b0:b0 + HD, h // 2, t * P:(t + 1) * P],
                                             kT[b0:b0 + HD, h // GROUP, :], start=True, stop=True)
                    m.then_inc(sc_full, 1)

                def prob_transposes(h):
                    pe.wait_ge(p_ready, l * HEADS + h + 1)
                    pe.wait_ge(pt_ready, l * HEADS + h + 1)
                    for i in range(4):
                        t, c = i // 2, i % 2
                        m = nc.tensor.transpose(ppt[:, i * P:(i + 1) * P], PR[:, h % 2, t, c * P:(c + 1) * P], ident[:, :])
                    m.then_inc(pt_full, 1)

                def values(h):
                    pe.wait_ge(pt_ready, l * HEADS + h + 2)
                    if h % 4 == 0:
                        pe.wait_ge(o_read, l * (HEADS // 4) + h // 4 + 1)
                    for t in range(NT):
                        o = po[:, (t * 4 + h % 4) * HD:(t * 4 + h % 4 + 1) * HD]
                        v0 = Q0 + KV0_V + (h // GROUP) * HD
                        for c in range(NT):
                            m = mm(o, PT[:, h % 2, t, c * P:(c + 1) * P], zrow[:, c, v0:v0 + HD],
                                                 start=(c == 0), stop=(c == 1))
                    m.then_inc(o_full, 1)

                KV0_V = 1024 + KV_HEADS * HD
                for s in range(16):
                    i = CC_S + s // 2
                    if s % 2 == 0:
                        weights(l, i)
                    if CX_S <= i < GA_S:
                        col_unit(bank_d(), i, s % 2, hT, pd_full, s % 2 == 1)
                    else:
                        col_unit(bank_a(), i, s % 2, hT, pa_full, s % 2 == 1)
                    if s >= 2:
                        values(s - 2)
                    if s >= 1:
                        prob_transposes(s - 1)
                    scores(s)
                for s in range(4):
                    i = CONVP_S + s // 2
                    if s % 2 == 0:
                        weights(l, i)
                    if s == 0:
                        pe.wait_ge(yconv_ready, l + 1)
                    col_unit(bank_d(), i, s % 2, cbT, pd_full, s % 2 == 1)
                    if s == 0:
                        values(HEADS - 2)
                        prob_transposes(HEADS - 1)
                    if s == 1:
                        values(HEADS - 1)
                pe.wait_ge(o_rows, (l + 1) * (HEADS // 4))
                for j in range(KC // 2):
                    b = bank_a()
                    for i in range(4):
                        c, t = 2 * j + i // 2, i % 2
                        m = nc.tensor.transpose(b[:, i * P:(i + 1) * P], orow[:, t, c * P:(c + 1) * P], ident[:, :])
                    m.then_inc(pa_full, 1)
                for s in range(4):
                    i = ATTNP_S + s // 2
                    if s % 2 == 0:
                        weights(l, i)
                    if s == 0:
                        pe.wait_ge(o_used, l + 1)
                    col_unit(bank_d(), i, s % 2, oT, pd_full, s % 2 == 1)

                def row_outputs(n, pieces, src):
                    for i, half, k0, nk in pieces:
                        weights(l, i)
                        for t in range(NT):
                            if k0 == 0:
                                pe.wait_ge(row_read, 4 * (2 * l + n) + 2 * half + t + 1)
                            for k in range(nk):
                                last = k0 + k == (FC if n else KC) - 1
                                m = mm(pr[2 * t + half][:, :], src[:, k0 + k, t * P:(t + 1) * P], slot(i)[:, k, :],
                                                     start=(k0 + k == 0), stop=last)
                            if last:
                                m.then_inc(row_full, 1)
                        used_up()

                pe.wait_ge(mix_ready, l + 1)
                row_outputs(0, [(OUT_S, 0, 0, KC), (OUT_S + 1, 1, 0, KC)], sga)
                norm_transposes(1)
                pe.wait_ge(hT_ready, 2 * l + 2)
                for i in range(FFN_S, DOWN_S):
                    weights(l, i)
                    for c in range(2):
                        b = bank_d()
                        for g in range(2):
                            for k in range(KC):
                                m = mm(b[:, g * SEQ:(g + 1) * SEQ], slot(i)[:, k, g * 256 + c * P:g * 256 + (c + 1) * P],
                                                     hT[:, k, :], start=(k == 0), stop=(k == KC - 1))
                        m.then_inc(pd_full, 1)
                    used_up()
                pe.wait_ge(f_ready, l + 1)
                row_outputs(1, [(DOWN_S + 3 * h + j, h, k0, k) for h in range(2) for j, (k0, k) in enumerate(DOWN_PIECES)], fT)
                assert owed[0] == 1
                pe.drain().then_inc(w_free, 1)
                assert (nd[0], na[0]) == (D_UNITS, A_UNITS)

            nd, na, owed = [DEPTH * D_UNITS], [DEPTH * A_UNITS], [0]

            def bank_d():
                u = nd[0]
                nd[0] += 1
                pe.wait_ge(pd_free, u + 1)
                return pd[u % 2]

            def bank_a():
                u = na[0]
                na[0] += 1
                pe.wait_ge(pa_free, u + 1)
                return pa[u % 2]

            def mm(out_, lhsT, rhs, start, stop):
                m = nc.tensor.matmul(out_, lhsT, rhs, start=start, stop=stop)
                if owed[0] and not stop:
                    m.then_inc(w_free, 1)
                    owed[0] -= 1
                return m

            def weights(j):
                pe.wait_ge(w_in_slot[j % R], DEPTH * LANDED_LAYER[j % R] + 16 * (j // R + 1))

            def row_unit(b, j, t, src, full):
                for k in range(KC):
                    m = mm(b[:, :], src[:, k, t * P:(t + 1) * P], slot(j)[:, k, :], k == 0, k == KC - 1)
                m.then_inc(full, 1)
                owed[0] += t

            def col_unit(b, j, half, src, full):
                for c in range(2):
                    for k in range(KC):
                        m = mm(b[:, c * SEQ:(c + 1) * SEQ], slot(j)[:, k, (2 * half + c) * P:(2 * half + c + 1) * P],
                               src[:, k, :], k == 0, k == KC - 1)
                m.then_inc(full, 1)
                owed[0] += half

            def to_columns(src, bank, full):
                for j in range(KC // 2):
                    b = bank()
                    for i in range(4):
                        c, t = 2 * j + i // 2, i % 2
                        m = nc.tensor.transpose(b[:, i * P:(i + 1) * P], src[:, t, c * P:(c + 1) * P], ident[:, :])
                    m.then_inc(full, 1)

            def gate_rows():
                pe.wait_ge(mod_ready, 1)
                for l in range(DEPTH):
                    for which in (2, 5):
                        for half in range(2):
                            b = bank_a()
                            for i in range(4):
                                c = (l * 6 + which) * KC + 4 * half + i
                                m = nc.tensor.matmul(b[:, i * P:(i + 1) * P], adac[:, c:c + 1].to_broadcast([P, P]), ident[:, :],
                                                     start=True, stop=True)
                            m.then_inc(pa_full, 1)

            def peer(l, j0):
                pe.wait_ge(xn_ready, 2 * DEPTH + 2 + 2 * l)
                to_columns(xn, bank_d, pd_full)
                pe.wait_ge(hT_ready, 2 * DEPTH + 2 + 2 * l)
                for t in range(NT):
                    for half in range(2):
                        b = bank_a()
                        for i in range(4):
                            m = nc.tensor.transpose(b[:, i * P:(i + 1) * P], hT[:, 4 * half + i, t * P:(t + 1) * P], ident[:, :])
                        m.then_inc(pa_full, 1)
                for s in range(8):
                    if s % 2 == 0:
                        weights(j0 + s // 2)
                    col_unit(bank_a(), j0 + s // 2, s % 2, hT, pa_full)
                pe.drain().then_inc(w_free, 1)
                owed[0] = 0
                pe.wait_ge(qp_ready, l + 1)
                pe.wait_ge(experts_in, 32 * (l + 1))
                for t in range(NT):
                    for q4 in range(4):
                        b = bank_a()
                        for i in range(4):
                            hp = 4 * q4 + i
                            m = nc.tensor.matmul(b[:, i * P:(i + 1) * P], qpT[:, hp, t * P:(t + 1) * P], keysT[:, hp % 2, :],
                                                 start=True, stop=True)
                        m.then_inc(pa_full, 1)

            gate_rows()
            pe.wait_ge(xn_ready, 2 * DEPTH + 1)
            to_columns(xn, bank_d, pd_full)
            pe.wait_ge(hT_ready, 2 * DEPTH + 1)
            for s in range(4):
                if s % 2 == 0:
                    weights(s // 2)
                col_unit(bank_d(), s // 2, s % 2, hT, pd_full)
            pe.wait_ge(lstm_in, 64)
            for g in range(2):
                for k in range(KC):
                    m = mm(pr[0][0:LSTM_HEADS, g * SEQ:(g + 1) * SEQ], wg[:, k, g * LSTM_HEADS:(g + 1) * LSTM_HEADS], hT[:, k, :],
                           k == 0, k == KC - 1)
            m.then_inc(if_full, 1)
            for j in range(2, 6):
                weights(j)
                for t in range(NT):
                    row_unit(bank_a(), j, t, hT, pa_full)
            pe.wait_ge(if_exp, 1)
            for i in range(4):
                src = (gg, gm)[i // 2]
                m = nc.tensor.transpose(pr[1][:, i * LSTM_HEADS:(i + 1) * LSTM_HEADS], src[:, (i % 2) * P:(i % 2 + 1) * P],
                                        ident[0:LSTM_HEADS, 0:LSTM_HEADS])
            m.then_inc(gcol_full, 1)
            pe.wait_ge(gcol_ready, 1)
            pe.wait_ge(qk_silu, KC // 2)
            pe.wait_ge(v_ready, 1)

            def lstm_scores(h):
                b0 = (h % 2) * LSTM_QK
                if h >= 2:
                    pe.wait_ge(m_read, h - 1)
                nc.tensor.matmul(pr[h % 2][:, 0:SEQ], ident[0:LSTM_HEADS, h:h + 1].to_broadcast([LSTM_HEADS, P]), gM[:, :],
                                 start=True, stop=True).then_inc(m_full, 1)
                if h >= 2:
                    pe.wait_ge(st_read, h - 1)
                k_, q_ = qkT[b0:b0 + LSTM_QK, KC // 2 + h // 2, :], qkT[b0:b0 + LSTM_QK, h // 2, :]
                nc.tensor.matmul(pr[2 + h % 2][:, 0:SEQ], k_[:, 0:P], q_, start=True, stop=True)
                nc.tensor.matmul(pr[2 + h % 2][:, SEQ:3 * P], k_[:, P:SEQ], q_[:, P:SEQ], start=True, stop=True).then_inc(st_full, 1)

            def lstm_values(h):
                pe.wait_ge(pl_ready, h + 1)
                b = bank_a()
                n = LSTM_V + 1
                nc.tensor.matmul(b[:, 0:n], Pl[:, h % 2, 0:P], vaug[:, 0, h, :], start=True, stop=True)
                nc.tensor.matmul(b[:, n:2 * n], Pl[:, h % 2, P:2 * P], vaug[:, 0, h, :], start=True, stop=False)
                nc.tensor.matmul(b[:, n:2 * n], Pl[:, h % 2, 2 * P:3 * P], vaug[:, 1, h, :], start=False, stop=True).then_inc(pa_full, 1)

            for h in range(LSTM_HEADS + 1):
                if h < LSTM_HEADS:
                    lstm_scores(h)
                if h:
                    lstm_values(h - 1)
            pe.wait_ge(y_rows, 1)
            to_columns(xn, bank_a, pa_full)
            pe.wait_ge(yT_ready, 1)
            for j in (6, 7):
                weights(j)
                for t in range(NT):
                    row_unit(bank_d(), j, t, hT, pd_full)
            peer(0, 8)

            pe.wait_ge(xn_ready, 2 * DEPTH + 3)
            to_columns(xn, bank_d, pd_full)
            pe.wait_ge(hT_ready, 2 * DEPTH + 3)
            for j in range(12, 18):
                weights(j)
                for t in range(NT):
                    row_unit(bank_a(), j, t, hkT if j < 16 else hT, pa_full)
            pe.wait_ge(sqk_ready, 1)
            to_columns(srow[:, 0], bank_a, pa_full)
            pe.wait_ge(sqk_ready, 2)
            to_columns(srow[:, 2], bank_a, pa_full)
            pe.wait_ge(sT_ready, 1)
            pe.wait_ge(stick_in, 80)

            def z_scores(h):
                b0 = (h % 2) * SB_DIM
                if h >= 2:
                    pe.wait_ge(z_read, h - 1)
                k_, q_ = skT[b0:b0 + SB_DIM, h // 2, :], sqT[b0:b0 + SB_DIM, h // 2, :]
                nc.tensor.matmul(pr[h % 2][:, 0:SEQ], k_[:, 0:P], q_, start=True, stop=True)
                nc.tensor.matmul(pr[h % 2][:, SEQ:3 * P], k_[:, P:SEQ], q_[:, P:SEQ], start=True, stop=True).then_inc(z_full, 1)

            def sums_after(h):
                pe.wait_ge(spm_ready, h + 1)
                if h >= 2:
                    pe.wait_ge(cum_read, h - 1)
                b, s_ = pr[2 + h % 2], sp_[:, h % 2, :]
                nc.tensor.matmul(b[:, 0:P], tri[:, :], s_[:, 0:P], start=True, stop=True)
                nc.tensor.matmul(b[:, P:2 * P], tri[:, :], s_[:, P:2 * P], start=True, stop=False)
                nc.tensor.matmul(b[:, P:2 * P], ones[:, :], s_[:, 2 * P:3 * P], start=False, stop=True)
                nc.tensor.matmul(b[:, 2 * P:3 * P], tri[:, :], s_[:, 2 * P:3 * P], start=True, stop=True).then_inc(cum_full, 1)

            held = [None, None]

            def stick_values(h):
                if h % 8 == 0:
                    held[0], held[1] = bank_a(), bank_a()
                pe.wait_ge(a_ready, h + 1)
                c = slice((h % 8) * SB_DIM, (h % 8 + 1) * SB_DIM)
                a_, v_ = ex[:, h % 2, :], srow[:, 1, :, h * SB_DIM:(h + 1) * SB_DIM]
                m0 = nc.tensor.matmul(held[0][:, c], a_[:, 0:P], v_[:, 0, :], start=True, stop=True)
                nc.tensor.matmul(held[1][:, c], a_[:, P:2 * P], v_[:, 0, :], start=True, stop=False)
                m = nc.tensor.matmul(held[1][:, c], a_[:, 2 * P:3 * P], v_[:, 1, :], start=False, stop=True)
                if h % 8 == 7:
                    m0.then_inc(pa_full, 1)
                    m.then_inc(pa_full, 1)
                else:
                    m.then_inc(a_used, 1)
            for h in range(SB_HEADS + 2):
                if h < SB_HEADS:
                    z_scores(h)
                if 1 <= h <= SB_HEADS:
                    sums_after(h - 1)
                if h >= 2:
                    stick_values(h - 2)
            pe.wait_ge(y_rows, 2)
            to_columns(xn, bank_a, pa_full)
            pe.wait_ge(yT_ready, 2)
            for j in (18, 19):
                weights(j)
                for t in range(NT):
                    row_unit(bank_d(), j, t, hT, pd_full)
            peer(1, 20)

        @block.scalar
        def _(act):
            act.sem_inc(pa_free, 2)
            act.wait_ge(c_in, 16)
            nc.scalar.activation(crow[:, :], crow[:, :], ACT.Silu).then_inc(c_ready, 1)
            act.wait_ge(x_in, 16)

            with act.Fori(0, DEPTH) as l:
                na = [0]

                def take():
                    u = na[0]
                    na[0] += 1
                    act.wait_ge(pa_full, l * A_UNITS + u + 1)
                    return pa[u % 2][:, :]

                def squares(n):
                    act.wait_ge(x_ready, 2 * l + n + 1)
                    for t in range(NT):
                        if t:
                            act.drain()
                        m = nc.scalar.activation(junk[:, :], x[:, t, :], ACT.Square, accum_out=ssx[:, t:t + 1])
                    m.then_inc(ss_ready, 1)
                    act.drain()

                def row_squares(n):
                    for half in range(2):
                        for t in range(NT):
                            act.wait_ge(row_full, 4 * (2 * l + n) + 2 * half + t + 1)
                            nc.scalar.activation(junk[:, (half) * 512:(half + 1) * 512], pr[2 * t + half][:, :], ACT.Square,
                                                 accum_out=ssm[:, t, half:half + 1]).then_inc(ssm_ready, 1)
                            act.drain()

                squares(0)
                for s in range(3):
                    for t in range(NT):
                        m = nc.scalar.copy(zrow[:, t, s * 512:(s + 1) * 512], take()).then_inc(pa_free, 1)
                act.drain()
                act.sem_inc(qk_ready, 1)
                for j in range(4):
                    nc.scalar.copy(cbT[:, 2 * j:2 * j + 2, :].rearrange("p c n -> p (c n)"), take()).then_inc(pa_free, 1)
                for j in range(4):
                    nc.scalar.copy(qT[:, 2 * j:2 * j + 2, :].rearrange("p c n -> p (c n)"), take()).then_inc(pa_free, 1)
                for j in range(2):
                    nc.scalar.copy(kT[:, 2 * j:2 * j + 2, :].rearrange("p c n -> p (c n)"), take()).then_inc(pa_free, 1)
                act.drain()
                act.sem_inc(qk_ready, 1)
                for s in range(16):
                    i = CC_S + s // 2
                    j = s % 4
                    dst = {0: ccT, 2: sga, 3: sgb}.get(s // 4)
                    if dst is not None:
                        func = ACT.Copy if dst is ccT else ACT.Sigmoid
                        d = dst[:, 2 * j:2 * j + 2, :].rearrange("p c n -> p (c n)")
                        nc.scalar.activation(d, take(), func).then_inc(pa_free, 1)
                        if dst is ccT:
                            act.drain()
                            act.sem_inc(cc_ready, 1)
                    for t in range(NT):
                        act.wait_ge(nm_ready, l * HEADS + s + 1)
                        nc.scalar.activation(PR[:, s % 2, t, :], S[:, s % 2, t, :], ACT.Exp, bias=nm[:, s, t:t + 1],
                                             accum_out=den[:, s, t:t + 1])
                    act.drain()
                    act.sem_inc(p_ready, 1)
                    if s % 4 == 3:
                        act.wait_ge(es_sum, l * 4 + s // 4 + 1)
                        nc.scalar.activation(es[:, :, :], es[:, :, :], ACT.Exp).then_inc(es_ready, 1)
                act.sem_inc(sig_ready, 1)
                for j in range(4):
                    nc.scalar.copy(oT[:, 2 * j:2 * j + 2, :].rearrange("p c n -> p (c n)"), take()).then_inc(pa_free, 1)
                act.drain()
                act.sem_inc(o_used, 1)
                row_squares(0)
                squares(1)
                for u in range(FC):
                    act.wait_ge(pd_full, l * D_UNITS + 20 + u + 1)
                    act.wait_ge(silu_free, l * FC + u + 1)
                    nc.scalar.activation(silu[:, u % 2, :], pd[u % 2][:, 0:SEQ], ACT.Silu).then_inc(silu_ready, 1)
                row_squares(1)
                assert na[0] == A_UNITS

            na = [DEPTH * A_UNITS]

            def take():
                u = na[0]
                na[0] += 1
                act.wait_ge(pa_full, u + 1)
                return pa[u % 2][:, :]

            def squares(n):
                act.wait_ge(x_ready, 2 * DEPTH + 1 + n)
                for t in range(NT):
                    if t:
                        act.drain()
                    m = nc.scalar.activation(junk[:, :], x[:, t, :], ACT.Square, accum_out=ssx[:, t:t + 1])
                m.then_inc(ss_ready, 1)
                act.drain()

            def flat(v):
                return v.rearrange("p c n -> p (c n)")

            def columns_out(dst, ready):
                for j in range(KC // 2):
                    nc.scalar.copy(flat(dst[:, 2 * j:2 * j + 2, :]), take()).then_inc(pa_free, 1)
                act.drain().then_inc(ready, 1)

            def peer(l):
                squares(1 + 2 * l)
                for t in range(NT):
                    for half in range(2):
                        nc.scalar.copy(hrow[:, t, half * 512:(half + 1) * 512], take()).then_inc(pa_free, 1)
                for s in range(8):
                    nc.scalar.copy(flat(qpT[:, 2 * s:2 * s + 2, :]), take()).then_inc(pa_free, 1)
                act.drain().then_inc(qp_ready, 1)
                for t in range(NT):
                    for q4 in range(4):
                        nc.scalar.copy(flat(sc[:, t, 4 * q4:4 * q4 + 4, :]), take()).then_inc(pa_free, 1)
                    act.drain().then_inc(sc_ready, 1)
                for t in range(NT):
                    act.wait_ge(g_arg, 2 * l + t + 1)
                    nc.scalar.activation(wexp[:, t], wexp[:, t], ACT.Exp).then_inc(g_exp, 1)
                for t in range(NT):
                    act.wait_ge(dots_ready, 2 * l + t + 1)
                    nc.scalar.activation(coef[:, :], dots[:, :], ACT.Gelu).then_inc(gelu_ready, 1)

            for half in range(8):
                nc.scalar.copy(grows[:, half // 2, (half % 2) * 512:(half % 2 + 1) * 512], take()).then_inc(pa_free, 1)
            act.drain().then_inc(grows_ready, 1)
            squares(0)
            act.wait_ge(if_abs, 1)
            nc.scalar.activation(ge[:, :], ge[:, :], ACT.Exp, scale=-1.0)
            act.drain()
            nc.scalar.activation(gl[:, :], ge[:, :], ACT.Ln, bias=1.0).then_inc(if_log, 1)
            for j in range(KC // 2):
                act.wait_ge(qk_pre, j + 1)
                nc.scalar.activation(qkT[:, 2 * j:2 * j + 2, :], qkT[:, 2 * j:2 * j + 2, :], ACT.Silu).then_inc(qk_silu, 1)
            for j in range(2):
                for t in range(NT):
                    nc.scalar.copy(vaug[:, t, 4 * j:4 * j + 4, 0:LSTM_V], take().rearrange("p (h v) -> p h v", v=LSTM_V)).then_inc(pa_free, 1)
            act.drain().then_inc(v_ready, 1)
            for j in range(2):
                for t in range(NT):
                    nc.scalar.activation(so[:, t, j * 512:(j + 1) * 512], take(), ACT.Sigmoid).then_inc(pa_free, 1)
            act.wait_ge(if_sum, 1)
            nc.scalar.activation(gm[:, :], gm[:, :], ACT.Exp, scale=-1.0).then_inc(if_exp, 1)
            for h in range(LSTM_HEADS + 1):
                if h < LSTM_HEADS:
                    act.wait_ge(d_pre, h + 1)
                    nc.scalar.activation(Dt[:, h % 2, :], Dt[:, h % 2, :], ACT.Exp, scale=-1.0).then_inc(d_ready, 1)
                if h:
                    nc.scalar.copy(numS[:, h - 1].rearrange("p t v -> p (t v)"), take()[:, 0:2 * (LSTM_V + 1)]).then_inc(pa_free, 1)
            act.drain().then_inc(num_ready, 1)
            columns_out(hT, yT_ready)
            peer(0)

            squares(2)
            for w in range(3):
                for j in range(2):
                    for t in range(NT):
                        nc.scalar.copy(srow[:, w, t, j * 512:(j + 1) * 512], take()).then_inc(pa_free, 1)
                act.drain().then_inc(srow_ready, 1)
            for dst in (skT, sqT):
                for j in range(KC // 2):
                    nc.scalar.copy(flat(dst[:, 2 * j:2 * j + 2, :]), take()).then_inc(pa_free, 1)
            act.drain().then_inc(sT_ready, 1)
            for h in range(SB_HEADS + 1):
                if h < SB_HEADS:
                    act.wait_ge(z_full, h + 1)
                    nc.scalar.activation(az[:, h % 2, :], pr[h % 2][:, 0:3 * P], ACT.Abs)
                    act.drain()
                    nc.scalar.activation(az[:, h % 2, :], az[:, h % 2, :], ACT.Exp, scale=-1.0)
                    act.drain()
                    nc.scalar.activation(sL[:, h % 2, :], az[:, h % 2, :], ACT.Ln, bias=1.0).then_inc(sL_ready, 1)
                if h:
                    act.wait_ge(ex_ready, h)
                    nc.scalar.activation(ex[:, (h - 1) % 2, :], ex[:, (h - 1) % 2, :], ACT.Exp).then_inc(a_exp, 1)
                if h >= 3 and (h - 3) % 8 == 7 or h == SB_HEADS:
                    g = 0 if h < SB_HEADS else 1
                    for t in range(NT):
                        nc.scalar.copy(xn[:, t, g * 512:(g + 1) * 512], take()).then_inc(pa_free, 1)
            act.drain().then_inc(y_rows, 1)
            columns_out(hT, yT_ready)
            peer(1)

        @block.gpsimd
        def _(pool):
            pool.wait_ge(c_ready, 1)
            with pool.Fori(0, ADA_CHUNKS // 2) as i:
                for a in range(2):
                    pool.wait_ge(ada_free, 2 * i + a + 1)
                    pool.sem_inc(wait_seen, 1)
                    pool.dma_start(aring[:, a, :], ins["ada_rows"][bass.ds(2 * i + a, 1)].rearrange("a p n -> p (a n)")).then_inc(ada_in[a], 16)
            for tt in range(DEPTH * NT):
                for phase, table in ((2 * tt, "peer_u"), (2 * tt + 1, "peer_v")):
                    with pool.Fori(0, TURNS) as i:
                        for a in range(2):
                            pool.wait_ge(ix_ready, 18 * tt + 8 * (phase % 2) + 2 * i + a + 1)
                            pool.sem_inc(wait_seen, 1)
                            for j in range(TOPK):
                                n = a * TOPK + j
                                pool.wait_ge(rows_free, phase * PICKS + i * PAIR + n + 1)
                                pool.sem_inc(wait_seen, 1)
                                pool.indirect_dma_start(out=gring[:, n % RING, :], out_offset=None, in_=ins[table],
                                                        in_offset=bass.IndirectOffsetOnAxis(ap=ix[:, a, j:j + 1], axis=0)).then_inc(row_in[n % RING], 16)

        @block.vector
        def _(dve):
            dve.sem_inc(pd_free, 2)
            dve.sem_inc(par_free, 2)
            dve.sem_inc(sc_read, 2)
            dve.sem_inc(pt_ready, 1)
            dve.sem_inc(o_read, 1)
            dve.sem_inc(row_read, 4)
            dve.sem_inc(silu_free, 2)
            nc.vector.memset(uT[:, :, 0:1], 0.0)
            nc.vector.memset(uT[:, :, SEQ + 1:SEQ + 2], 0.0)
            dve.wait_ge(const_in, 48)
            dve.wait_ge(x_in, 16)
            dve.sem_inc(x_ready, 1)
            dve.drain()

            def rsqrt(y, total, n, eps=EPS):
                w = total.shape[1]
                v, a = rsv[:, 0:w], rsa[:, 0:w]
                y, total = y[:, 0:w], total[:, 0:w]
                nc.vector.tensor_scalar(v, total, 1.0 / n, eps, ALU.mult, ALU.add)
                dve.drain()
                nc.vector.tensor_scalar(a.bitcast(I32), v.bitcast(I32), 1, None, ALU.arith_shift_right)
                dve.drain()
                nc.vector.tensor_scalar(y.bitcast(I32), a.bitcast(I32), -1.0, float(0x5F3759DF), ALU.mult, ALU.add)
                dve.drain()
                for _ in range(3):
                    nc.vector.scalar_tensor_tensor(a, y, -0.5, y, ALU.mult, ALU.mult)
                    dve.drain()
                    nc.vector.tensor_tensor(a, a, v, ALU.mult)
                    dve.drain()
                    nc.vector.scalar_tensor_tensor(y, a, 1.5, y, ALU.add, ALU.mult)
                    dve.drain()

            dve.sem_inc(ada_free, 2)
            dve.sem_inc(rows_free, RING)
            with dve.Fori(0, DEPTH) as l:
                nd = [0]
                nada = [0]

                def modulation(n):
                    for _ in range(n):
                        j = nada[0]
                        nada[0] += 1
                        dve.wait_ge(ada_in[j % 2], 16 * (ADA_LAYER // 2) * l + 16 * (j // 2) + 16)
                        nc.vector.tensor_tensor_reduce(out=aring[:, j % 2, :], in0=aring[:, j % 2, :], in1=crow[:, :], scale=1.0, scalar=0.0,
                                                       op0=ALU.mult, op1=ALU.add, accum_out=adal[:, j:j + 1]).then_inc(ada_free, 1)

                def take():
                    u = nd[0]
                    nd[0] += 1
                    dve.wait_ge(pd_full, l * D_UNITS + u + 1)
                    return pd[u % 2]

                def norm(n, g):
                    dve.wait_ge(ss_ready, 2 * l + n + 1)
                    rsqrt(rsx, ssx, D)
                    for t in range(NT):
                        nc.vector.tensor_scalar(xn[:, t, :], x[:, t, :], rsx[:, t:t + 1], None, ALU.mult)
                    dve.drain()
                    dve.sem_inc(xn_ready, 1)
                    for j in range(KC // 2):
                        b = take()
                        gb = cols[:, g + 2 * j:g + 2 * j + 2].unsqueeze(2).to_broadcast([P, 2, SEQ])
                        nc.vector.tensor_tensor(hT[:, 2 * j:2 * j + 2, :], b[:, :].rearrange("p (c n) -> p c n", c=2), gb,
                                                ALU.mult).then_inc(pd_free, 1)
                    dve.drain()
                    dve.sem_inc(hT_ready, 1)

                def add_rows(n):
                    dve.wait_ge(ssm_ready, 4 * (2 * l + n) + 4)
                    nc.vector.tensor_tensor(rsm[:, :], ssm[:, :, 0], ssm[:, :, 1], ALU.add)
                    dve.drain()
                    rsqrt(rsm, rsm, D)
                    for half in range(2):
                        for t in range(NT):
                            cut = slice(half * 512, (half + 1) * 512)
                            nc.vector.scalar_tensor_tensor(xn[:, t, cut], pr[2 * t + half][:, :], rsm[:, t:t + 1],
                                                           rows[:, n, cut], ALU.mult, ALU.mult).then_inc(row_read, 1)
                    dve.drain()
                    for t in range(NT):
                        nc.vector.tensor_tensor(x[:, t, :], x[:, t, :], xn[:, t, :], ALU.add)
                    dve.drain()
                    dve.sem_inc(x_ready, 1)

                dve.wait_ge(par_in, 64 * l + 64)
                norm(0, G_PRE)
                dve.wait_ge(qk_ready, 2 * l + 1)
                HK = HEADS + KV_HEADS
                heads = zrow[:, :, 0:HK * HD].rearrange("p t (h d) -> p t h d", d=HD)
                x1, x2 = heads[:, :, :, 0:HALF], heads[:, :, :, HALF:ROT]
                tmp = [rt[:, i, :].rearrange("p (t h d) -> p t h d", t=NT, d=HALF) for i in range(4)]
                cosb = cs[:, 0, :, :].unsqueeze(2).to_broadcast([P, NT, HK, HALF])
                sinb = cs[:, 1, :, :].unsqueeze(2).to_broadcast([P, NT, HK, HALF])
                nc.vector.tensor_tensor(tmp[0], x1, cosb, ALU.mult)
                nc.vector.tensor_tensor(tmp[1], x2, sinb, ALU.mult)
                nc.vector.tensor_tensor(tmp[2], x2, cosb, ALU.mult)
                nc.vector.tensor_tensor(tmp[3], x1, sinb, ALU.mult)
                dve.drain()
                nc.vector.tensor_tensor(x1, tmp[0], tmp[1], ALU.subtract)
                nc.vector.tensor_tensor(x2, tmp[2], tmp[3], ALU.add)
                dve.drain()
                for t in range(NT):
                    for a in range(2):
                        nc.vector.tensor_copy(kdup[:, t, :, a, :], zrow[:, t, HEADS * HD:HK * HD].rearrange("p (g d) -> p g d", d=HD))
                dve.drain()
                dve.sem_inc(rope_done, 1)

                def values_out(g):
                    dve.wait_ge(o_full, l * HEADS + 4 * g + 4)
                    dve.wait_ge(es_ready, l * 4 + g + 1)
                    nc.vector.tensor_tensor(es[:, :, :], es[:, :, :], den[:, 4 * g:4 * g + 4, :], ALU.add)
                    dve.drain()
                    nc.vector.reciprocal(rden[:, :, :], es[:, :, :].rearrange("p h t -> p t h"))
                    dve.drain()
                    for t in range(NT):
                        nc.vector.tensor_tensor(orow[:, t, 4 * g * HD:4 * (g + 1) * HD].rearrange("p (h d) -> p h d", d=HD),
                                                po[:, t * 256:(t + 1) * 256].rearrange("p (h d) -> p h d", d=HD),
                                                rden[:, t, :].unsqueeze(2).to_broadcast([P, 4, HD]), ALU.mult)
                    dve.drain()
                    dve.sem_inc(o_read, 1)
                    dve.sem_inc(o_rows, 1)

                def softmax_max(h):
                    dve.wait_ge(sc_full, l * HEADS + h + 1)
                    dve.sem_inc(sc_seen, 1)
                    for t in range(NT):
                        nc.vector.tensor_tensor_reduce(out=S[:, h % 2, t, :], in0=psc[h % 2][:, t * SEQ:(t + 1) * SEQ],
                                                       in1=mask8[:, t, :], scale=HD ** -0.5, scalar=-3e38,
                                                       op0=ALU.add, op1=ALU.max, accum_out=rmx[:, h, t:t + 1])
                    dve.drain()
                    dve.sem_inc(sc_read, 1)
                    nc.vector.tensor_scalar(nm[:, h, :], rmx[:, h, :], sinks[:, h:h + 1], -1.0, ALU.max, ALU.mult)
                    dve.drain()
                    dve.sem_inc(nm_ready, 1)

                def probs_out(h):
                    dve.wait_ge(pt_full, l * HEADS + h + 1)
                    nc.vector.tensor_copy(PT[:, h % 2, :, :].rearrange("p t n -> p (t n)"), ppt[:, :])
                    dve.drain()
                    dve.sem_inc(pt_ready, 1)

                def conv(j):
                    b = take()
                    dve.wait_ge(cc_ready, 4 * l + j + 1)
                    nc.vector.tensor_tensor(uT[:, 2 * j:2 * j + 2, 1:SEQ + 1], b[:, :].rearrange("p (c n) -> p c n", c=2),
                                            ccT[:, 2 * j:2 * j + 2, :], ALU.mult).then_inc(pd_free, 1)
                    dve.drain()
                    for k in range(3):
                        for c in range(2):
                            cc = 2 * j + c
                            w = cols[:, CONVW + 3 * cc + k:CONVW + 3 * cc + k + 1]
                            if k == 0:
                                nc.vector.tensor_scalar(cvt[:, c, :], uT[:, cc, 0:SEQ], w, None, ALU.mult)
                            else:
                                nc.vector.scalar_tensor_tensor(cvt[:, c, :], uT[:, cc, k:k + SEQ], w, cvt[:, c, :], ALU.mult, ALU.add)
                        dve.drain()
                    nc.vector.tensor_tensor(cbT[:, 2 * j:2 * j + 2, :], cbT[:, 2 * j:2 * j + 2, :], cvt[:, :, :], ALU.mult)
                    dve.drain()

                for s in range(16):
                    if s >= 4:
                        modulation(1)
                    if 4 <= s < 8:
                        conv(s - 4)
                    if s == 8:
                        dve.sem_inc(yconv_ready, 1)
                    if s >= 2 and (s - 2) % 4 == 3:
                        values_out((s - 2) // 4)
                    if s >= 1:
                        probs_out(s - 1)
                    softmax_max(s)
                    if s % 4 == 3:
                        nc.vector.tensor_tensor(es[:, :, :], nm[:, s - 3:s + 1, :], sinks[:, s - 3:s + 1].unsqueeze(2).to_broadcast([P, 4, NT]), ALU.add)
                        dve.drain()
                        dve.sem_inc(es_sum, 1)
                for j in range(4):
                    b = take()
                    if j == 0:
                        dve.wait_ge(sig_ready, l + 1)
                    v = sgb[:, 2 * j:2 * j + 2, :].rearrange("p c n -> p (c n)")
                    nc.vector.tensor_tensor(v, b[:, :], v, ALU.mult).then_inc(pd_free, 1)
                    if j == 0:
                        probs_out(HEADS - 1)
                values_out(3)
                for j in range(4):
                    b = take()
                    v = sga[:, 2 * j:2 * j + 2, :].rearrange("p c n -> p (c n)")
                    w = sgb[:, 2 * j:2 * j + 2, :].rearrange("p c n -> p (c n)")
                    nc.vector.tensor_tensor(v, b[:, :], v, ALU.mult).then_inc(pd_free, 1)
                    dve.drain()
                    nc.vector.tensor_tensor(v, v, w, ALU.add)
                dve.drain()
                dve.sem_inc(mix_ready, 1)
                add_rows(0)
                norm(1, G_FFN)
                for u in range(FC):
                    b = take()
                    dve.wait_ge(silu_ready, l * FC + u + 1)
                    nc.vector.tensor_tensor(fT[:, u, :], b[:, SEQ:2 * SEQ], silu[:, u % 2, :], ALU.mult).then_inc(pd_free, 1)
                    dve.drain()
                    dve.sem_inc(silu_free, 1)
                    modulation(2)
                dve.sem_inc(f_ready, 1)
                add_rows(1)
                dve.sem_inc(par_free, 2)
                nc.vector.tensor_copy(adac[:, bass.ds(l * ADA_LAYER, ADA_LAYER)], adal[:, :])
                dve.drain()
                assert (nd[0], nada[0]) == (D_UNITS, ADA_LAYER)

            nd = [DEPTH * D_UNITS]

            def take():
                u = nd[0]
                nd[0] += 1
                dve.wait_ge(pd_full, u + 1)
                return pd[u % 2]

            dve.wait_ge(cols2_in, 32)
            nc.vector.tensor_tensor(adac[:, :], adac[:, :], adab[:, :], ALU.add)
            dve.drain()

            def shift(n):
                c = KV_ADA if n == 4 else ((n // 2) * 6 + 3 * (n % 2)) * KC
                return adac[:, c:c + KC]

            for n in range(5):
                c = KV_ADA + KC if n == 4 else ((n // 2) * 6 + 3 * (n % 2) + 1) * KC
                g = N_KV if n == 4 else (N_MIX, N_FFN)[n % 2] + (n // 2) * KC
                nc.vector.scalar_tensor_tensor(modA[:, n, :], adac[:, c:c + KC], 1.0, cols2[:, g:g + KC], ALU.add, ALU.mult)
            dve.drain()
            dve.sem_inc(mod_ready, 1)

            def norm(n, outs):
                dve.wait_ge(ss_ready, 2 * DEPTH + n + 1)
                rsqrt(rsx, ssx, D)
                for t in range(NT):
                    nc.vector.tensor_scalar(xn[:, t, :], x[:, t, :], rsx[:, t:t + 1], None, ALU.mult)
                dve.drain()
                dve.sem_inc(xn_ready, 1)
                for j in range(KC // 2):
                    b = take()
                    for m, dst in outs:
                        for i in range(2):
                            c = 2 * j + i
                            nc.vector.tensor_scalar(dst[:, c, :], b[:, i * SEQ:(i + 1) * SEQ], modA[:, m, c:c + 1], shift(m)[:, c:c + 1],
                                                    ALU.mult, ALU.add)
                    dve.drain()
                    dve.sem_inc(pd_free, 1)
                dve.sem_inc(hT_ready, 1)

            def add_gated(g):
                for half in range(2):
                    for t in range(NT):
                        cut = slice(half * 512, (half + 1) * 512)
                        b = take()
                        nc.vector.tensor_tensor(xn[:, t, cut], b[:, :], grows[:, g, cut], ALU.mult).then_inc(pd_free, 1)
                dve.drain()
                for t in range(NT):
                    nc.vector.tensor_tensor(x[:, t, :], x[:, t, :], xn[:, t, :], ALU.add)
                dve.drain()
                dve.sem_inc(x_ready, 1)

            def head_norm(v, sq, ss, rs, gain, n, scale):
                nc.vector.tensor_tensor(sq, v, v, ALU.mult)
                dve.drain()
                nc.vector.tensor_reduce(ss, sq.rearrange("p (h d) -> p h d", d=n), AX.X, ALU.add)
                dve.drain()
                rsqrt(rs, ss, n)
                v3 = v.rearrange("p (h d) -> p h d", d=n)
                nc.vector.tensor_tensor(v3, v3, rs.unsqueeze(2).to_broadcast([P, rs.shape[1], n]), ALU.mult)
                dve.drain()

            norm(0, [(0, hT)])
            dve.wait_ge(lstm_in, 64)
            nc.vector.memset(preT[:, :, 0:LSTM_CONV - 1], 0.0)
            nc.vector.memset(vaug[:, :, :, LSTM_V:LSTM_V + 1], 1.0)
            nc.vector.memset(gone[:, :], 1.0)
            for j in range(KC // 2):
                b = take()
                nc.vector.tensor_copy(preT[:, 2 * j:2 * j + 2, LSTM_CONV - 1:], b[:, :].rearrange("p (c n) -> p c n", c=2)).then_inc(pd_free, 1)
            dve.drain()
            dve.wait_ge(if_full, 1)
            nc.vector.tensor_scalar(gi[:, :], pr[0][0:LSTM_HEADS, 0:SEQ], bif[:, 0:1], None, ALU.add)
            nc.vector.tensor_scalar(gf[:, :], pr[0][0:LSTM_HEADS, SEQ:2 * SEQ], bif[:, 1:2], None, ALU.add)
            dve.drain()
            nc.vector.scalar_tensor_tensor(ge[:, :], gf[:, :], -1.0, gf[:, :], ALU.mult, ALU.max)
            dve.drain()
            dve.sem_inc(if_abs, 1)
            for j in range(KC // 2):
                for k in range(LSTM_CONV):
                    for c in range(2):
                        cc = 2 * j + c
                        w = cols2[:, LCONV + LSTM_CONV * cc + k:LCONV + LSTM_CONV * cc + k + 1]
                        dst = qkT[:, cc, :] if k == LSTM_CONV - 1 else lcv[:, c, :]
                        if k == 0:
                            nc.vector.tensor_scalar(dst, preT[:, cc, 0:SEQ], w, None, ALU.mult)
                        else:
                            nc.vector.scalar_tensor_tensor(dst, preT[:, cc, k:k + SEQ], w, lcv[:, c, :], ALU.mult, ALU.add)
                    dve.drain()
                dve.sem_inc(qk_pre, 1)
            dve.wait_ge(if_log, 1)
            nc.vector.scalar_tensor_tensor(gf[:, :], gf[:, :], 0.0, gl[:, :], ALU.min, ALU.subtract)
            dve.drain()
            nc.vector.tensor_tensor_scan(gb_[:, :], gone[:, :], gf[:, :], 0.0, ALU.mult, ALU.add)
            dve.drain()
            nc.vector.tensor_tensor(gg[:, :], gi[:, :], gb_[:, :], ALU.subtract)
            dve.drain()
            nc.vector.tensor_tensor_scan(gM[:, :], gg[:, :], gg[:, :], 0.0, ALU.max, ALU.max)
            dve.drain()
            nc.vector.tensor_tensor(gm[:, :], gb_[:, :], gM[:, :], ALU.add)
            dve.drain()
            dve.sem_inc(if_sum, 1)
            dve.wait_ge(gcol_full, 1)
            nc.vector.tensor_copy(gcol[:, :, :].rearrange("p a h -> p (a h)"), pr[1][:, 0:4 * LSTM_HEADS])
            dve.drain()
            dve.sem_inc(gcol_ready, 1)
            for h in range(LSTM_HEADS):
                dve.wait_ge(m_full, h + 1)
                for s_, (a0, a1, m0) in enumerate(((0, SEQ, 0), (SEQ, 3 * P, P))):
                    nc.vector.scalar_tensor_tensor(Dt[:, h % 2, a0:a1], pr[h % 2][:, m0:SEQ], gcol[:, s_, h:h + 1], biglm[:, a0:a1],
                                                   ALU.subtract, ALU.max)
                dve.drain()
                dve.sem_inc(d_pre, 1)
                dve.sem_inc(m_read, 1)
                dve.wait_ge(d_ready, h + 1)
                dve.wait_ge(st_full, h + 1)
                nc.vector.scalar_tensor_tensor(Pl[:, h % 2, :], pr[2 + h % 2][:, 0:3 * P], LSTM_QK ** -0.5, Dt[:, h % 2, :], ALU.mult, ALU.mult)
                dve.drain()
                dve.sem_inc(st_read, 1)
                dve.sem_inc(pl_ready, 1)
            dve.wait_ge(num_ready, 1)
            nc.vector.scalar_tensor_tensor(dcol[:, :, :], numS[:, :, :, LSTM_V], -1.0, numS[:, :, :, LSTM_V], ALU.mult, ALU.max)
            dve.drain()
            nc.vector.tensor_tensor(dcol[:, :, :], dcol[:, :, :], gcol[:, 2:4, :].rearrange("p t h -> p h t"), ALU.max)
            dve.drain()
            nc.vector.reciprocal(dcol[:, :, :], dcol[:, :, :])
            dve.drain()
            for t in range(NT):
                nc.vector.tensor_tensor(xn[:, t, :].rearrange("p (h v) -> p h v", v=LSTM_V), numS[:, :, t, 0:LSTM_V],
                                        dcol[:, :, t].unsqueeze(2).to_broadcast([P, LSTM_HEADS, LSTM_V]), ALU.mult)
            dve.drain()
            flat_xn = xn[:, :, :].rearrange("p t n -> p (t n)")
            head_norm(flat_xn, numS[:, :, :, :].rearrange("p h t v -> p (h t v)")[:, 0:NT * D], rsb[:, 0:16], rcol[:, :], None, LSTM_V, 1.0)
            nc.vector.tensor_tensor(xn[:, :, :], xn[:, :, :], hng[:, :].unsqueeze(1).to_broadcast([P, NT, D]), ALU.mult)
            dve.drain()
            nc.vector.tensor_tensor(xn[:, :, :], xn[:, :, :], so[:, :, :], ALU.mult)
            dve.drain()
            dve.sem_inc(y_rows, 1)
            dve.wait_ge(grows_ready, 1)
            add_gated(0)

            def top16(src, spare, vals, idxs, n):
                for i in range(n):
                    nc.vector.max(vals(i)[:, 0:8], src(i))
                dve.drain()
                for i in range(n):
                    nc.vector.max_index(idxs(i)[:, 0:8], vals(i)[:, 0:8], src(i))
                    nc.vector.match_replace(spare(i), vals(i)[:, 0:8], src(i), -3e38)
                dve.drain()
                for i in range(n):
                    nc.vector.max(vals(i)[:, 8:16], spare(i))
                dve.drain()
                for i in range(n):
                    nc.vector.max_index(idxs(i)[:, 8:16], vals(i)[:, 8:16], spare(i))
                dve.drain()

            def choose(l, t):
                dve.wait_ge(sc_ready, 2 * l + 2)
                if t == 0:
                    dve.wait_ge(experts_in, 32 * (l + 1))
                top16(lambda i: sc[:, t, i, :], lambda i: sc2[:, i, :], lambda i: top[:, i // 2, i % 2, :],
                      lambda i: topi[:, i // 2, i % 2, :], 2 * PEER_HEADS)
                nc.vector.tensor_copy(topf[:, :, :, :], topi[:, :, :, :])
                shape = [P, PEER_HEADS, TOPK, TOPK]
                c4 = cand.rearrange("p h (i j) -> p h i j", j=TOPK)
                nc.vector.tensor_tensor(c4, top[:, :, 0, :].unsqueeze(3).to_broadcast(shape), top[:, :, 1, :].unsqueeze(2).to_broadcast(shape), ALU.add)
                dve.drain()
                spare = sc2[:, :, :].rearrange("p (h a) n -> p h (a n)", a=2)
                top16(lambda i: cand[:, i, :], lambda i: spare[:, i, :], lambda i: gt[:, i, :], lambda i: pos[:, i, :], PEER_HEADS)
                nc.vector.tensor_tensor(wexp[:, t], gt[:, :, :], gt[:, :, 0:1].to_broadcast([P, PEER_HEADS, TOPK]), ALU.subtract)
                dve.drain()
                dve.sem_inc(g_arg, 1)
                pf = pos[:, :, :].rearrange("p h k -> p (h k)")
                nc.vector.tensor_scalar(hilo[:, 0, :], pf, 4, None, ALU.logical_shift_right)
                nc.vector.tensor_scalar(hilo[:, 1, :], pf, 15, None, ALU.bitwise_and)
                dve.drain()
                nc.vector.tensor_copy(hilof[:, :, :], hilo[:, :, :])
                dve.drain()
                for a in range(2):
                    p3 = pick.rearrange("p h (k i) -> p (h k) i", i=TOPK)
                    p4 = pick.rearrange("p h (k i) -> p h k i", i=TOPK)
                    nc.vector.tensor_tensor(p3, hilof[:, a, :].unsqueeze(2).to_broadcast([P, PICKS, TOPK]),
                                            iota[:, :].unsqueeze(1).to_broadcast([P, PICKS, TOPK]), ALU.is_equal)
                    dve.drain()
                    nc.vector.tensor_tensor(p4, p4, topf[:, :, a, :].unsqueeze(2).to_broadcast(shape), ALU.mult)
                    dve.drain()
                    nc.vector.tensor_reduce(ef[:, a, :], p3, AX.X, ALU.add)
                    dve.drain()
                nc.vector.tensor_scalar(ef[:, 0, :], ef[:, 0, :], float(NKEYS), float(l * EXPERTS), ALU.mult, ALU.add)
                dve.drain()
                nc.vector.tensor_tensor(eidx[:, t, 0:PICKS], ef[:, 0, :], ef[:, 1, :], ALU.add)
                dve.drain()
                nc.vector.tensor_copy(eidx[:, t, PICKS:PICKS + PAIR], eidx[:, t, 0:PAIR])
                dve.wait_ge(g_exp, 2 * l + t + 1)
                nc.vector.tensor_reduce(wsum[:, :], wexp[:, t], AX.X, ALU.add)
                dve.drain()
                nc.vector.reciprocal(wsum[:, :], wsum[:, :])
                dve.drain()
                nc.vector.tensor_tensor(wexp[:, t], wexp[:, t], wsum[:, :].unsqueeze(2).to_broadcast([P, PEER_HEADS, TOPK]), ALU.mult)
                dve.drain()

            def landed_row(phase, i, n):
                dve.wait_ge(row_in[n % RING], 16 * (PICKS // RING) * phase + i * (16 * PAIR // RING) + 16 * (n // RING + 1))

            def next_picks(t, i, a):
                nc.vector.tensor_copy(ix[:, a, :], eidx[:, t, bass.ds(i * PAIR + PAIR + a * TOPK, TOPK)])
                dve.drain()
                dve.sem_inc(ix_ready, 1)

            def expert_rows(l, t):
                tt = 2 * l + t
                for a in range(2):
                    nc.vector.tensor_copy(ix[:, a, :], eidx[:, t, a * TOPK:(a + 1) * TOPK])
                    dve.drain()
                    dve.sem_inc(ix_ready, 1)
                with dve.Fori(0, TURNS) as i:
                    for a in range(2):
                        for j in range(TOPK):
                            n = a * TOPK + j
                            landed_row(2 * tt, i, n)
                            nc.vector.tensor_tensor_reduce(out=gring[:, n % RING, :], in0=gring[:, n % RING, :], in1=hrow[:, t, :], scale=1.0,
                                                           scalar=0.0, op0=ALU.mult, op1=ALU.add,
                                                           accum_out=a16[:, a, j:j + 1]).then_inc(rows_free, 1)
                        dve.drain()
                        nc.vector.tensor_copy(dots[:, bass.ds(i * PAIR + a * TOPK, TOPK)], a16[:, a, :])
                        next_picks(t, i, a)
                dve.sem_inc(dots_ready, 1)
                nc.vector.memset(acc[:, :], 0.0)
                dve.wait_ge(gelu_ready, tt + 1)
                nc.vector.tensor_tensor(coef[:, :], coef[:, :], wexp[:, t].rearrange("p h k -> p (h k)"), ALU.mult)
                dve.drain()
                with dve.Fori(0, TURNS) as i:
                    for a in range(2):
                        for j in range(TOPK):
                            n = a * TOPK + j
                            landed_row(2 * tt + 1, i, n)
                            nc.vector.scalar_tensor_tensor(acc[:, :], gring[:, n % RING, :], coef[:, bass.ds(i * PAIR + n, 1)], acc[:, :],
                                                           ALU.mult, ALU.add).then_inc(rows_free, 1)
                            dve.drain()
                        next_picks(t, i, a)
                nc.vector.tensor_tensor(acc[:, :], acc[:, :], grows[:, 2 * l + 1, :], ALU.mult)
                dve.drain()
                nc.vector.tensor_tensor(x[:, t, :], x[:, t, :], acc[:, :], ALU.add)
                dve.drain()

            def peer(l):
                norm(1 + 2 * l, [(2 * l + 1, hT)])
                for t in range(NT):
                    choose(l, t)
                for t in range(NT):
                    expert_rows(l, t)
                dve.sem_inc(x_ready, 1)

            peer(0)

            norm(2, [(2, hT), (4, hkT)])
            dve.wait_ge(stick_in, 80)
            for n, (w, scale) in enumerate(((0, 1.0), (2, SB_DIM ** -0.5))):
                dve.wait_ge(srow_ready, w + 1)
                v = srow[:, w].rearrange("p t n -> p (t n)")
                head_norm(v, sqs[:, :, :].rearrange("p t n -> p (t n)"), sss[:, :], srs[:, :], None, SB_DIM, 1.0)
                v3 = v.rearrange("p (h d) -> p h d", d=SB_DIM)
                nc.vector.scalar_tensor_tensor(v3, v3, scale, qkg[:, n, :].unsqueeze(1).to_broadcast([P, NT * SB_HEADS, SB_DIM]), ALU.mult, ALU.mult)
                dve.drain()
                dve.sem_inc(sqk_ready, 1)
            for h in range(SB_HEADS + 1):
                if h < SB_HEADS:
                    z, r = pr[h % 2][:, 0:3 * P], h % 2
                    dve.wait_ge(z_full, h + 1)
                    dve.wait_ge(sL_ready, h + 1)
                    if h >= 2:
                        dve.wait_ge(cum_full, h - 1)
                    nc.vector.scalar_tensor_tensor(sp_[:, r, :], z, 0.0, sL[:, r, :], ALU.max, ALU.add)
                    nc.vector.scalar_tensor_tensor(ls[:, r, :], z, 0.0, sL[:, r, :], ALU.min, ALU.subtract)
                    dve.drain()
                    dve.sem_inc(z_read, 1)
                    nc.vector.tensor_tensor(sp_[:, r, :], sp_[:, r, :], strict[:, :], ALU.mult)
                    dve.drain()
                    dve.sem_inc(spm_ready, 1)
                if h:
                    r = (h - 1) % 2
                    dve.wait_ge(cum_full, h)
                    if h >= 3:
                        if (h - 3) % 8 == 7:
                            dve.wait_ge(pa_full, STICK_FULL)
                        else:
                            dve.wait_ge(a_used, (h - 3) + 1 - (h - 3) // 8)
                    nc.vector.tensor_tensor(ex[:, r, :], ls[:, r, :], pr[2 + r][:, 0:3 * P], ALU.subtract)
                    dve.drain()
                    dve.sem_inc(cum_read, 1)
                    dve.sem_inc(ex_ready, 1)
                    dve.wait_ge(a_exp, h)
                    nc.vector.tensor_tensor(ex[:, r, :], ex[:, r, :], strict[:, :], ALU.mult)
                    dve.drain()
                    dve.sem_inc(a_ready, 1)
            add_gated(2)
            peer(1)


def tables():
    q = np.arange(SEQ)
    far = np.abs(q[:, None] - q[None, :]) > WINDOW
    mask8 = np.where(far, np.float32(NEG / HD ** -0.5), np.float32(0.0)).astype(np.float32)
    i = np.arange(P)
    big = np.where(i[:, None] <= i[None, :], np.float32(0.0), np.float32(-NEG)).astype(np.float32)
    before = (i[:, None] < i[None, :]).astype(np.float32)
    inv = np.power(np.float32(THETA), -np.arange(0, ROT, 2, dtype=np.float32) / np.float32(ROT)).astype(np.float32)
    ang = np.arange(SEQ, dtype=np.float32)[:, None] * inv[None, :]
    cs = np.stack([np.cos(ang), np.sin(ang)]).astype(np.float32)
    return {
        "c_ident": np.eye(P, dtype=np.float32),
        "c_biglm": np.concatenate([big, np.zeros((P, P), np.float32), big], axis=1),
        "c_strict": np.concatenate([before, np.ones((P, P), np.float32), before], axis=1),
        "c_tri": (i[:, None] > i[None, :]).astype(np.float32),
        "c_ones": np.ones((P, P), np.float32),
        "c_iota": np.tile(np.arange(TOPK, dtype=np.float32), (P, 1)),
        "c_mask8": np.ascontiguousarray(mask8.reshape(NT, P, SEQ).transpose(1, 0, 2)),
        "c_cs": np.ascontiguousarray(cs.reshape(2, NT, P, HALF).transpose(2, 0, 1, 3)),
    }


def columns(a):
    return a.reshape(a.shape[:-1] + (-1, P)).swapaxes(-1, -2)


AS_THEY_COME = ["x", "w_in", "attn_sink", "w_attn_proj", "w_conv_proj", "w_out", "g_post_mix",
                "w_gate", "w_up", "w_down", "g_post_ffn", "c_2", "ma_w_in_2", "ma_w_out_2", "kv_w_2", "k_norm_g_2",
                "sb_w_q_2", "sb_q_norm_g_2", "sb_w_out_2", "peer_w_q_2"]


def kernel(**inputs):
    import concourse.bacc as bacc
    from concourse.bass_utils import run_bass_kernel_spmd as run

    a = {k: np.asarray(v) for k, v in inputs.items()}
    sent = {k: a[k] for k in AS_THEY_COME}
    conv = a["conv_w"].reshape(DEPTH, 3, KC, P).transpose(0, 3, 2, 1).reshape(DEPTH, P, KC * 3)
    sent["cols_a"] = np.concatenate([columns(a["g_pre_mix"]), columns(a["g_pre_ffn"]), conv], axis=2)
    lconv = a["ma_conv_w_2"][0].reshape(LSTM_CONV, KC, P).transpose(2, 1, 0).reshape(P, KC * LSTM_CONV)
    sent["cols_b"] = np.concatenate([columns(a["norm_mix_g_2"].reshape(-1)), columns(a["norm_ffn_g_2"].reshape(-1)),
                                     columns(a["kv_norm_g_2"]), lconv], axis=1)
    sent["ada_bias"] = columns(np.concatenate([a["ada_b_2"].reshape(-1), a["kv_ada_b_2"]]))
    sent["ada_rows"] = np.concatenate([a["ada_w_2"].transpose(0, 2, 1).reshape(-1, P, D), a["kv_ada_w_2"].T.reshape(-1, P, D)])
    sent["b_if"] = a["ma_b_if_2"].reshape(2, LSTM_HEADS).T
    sent["hnorm"] = a["ma_hnorm_g_2"].reshape(1, D)
    sent["keysT"] = a["peer_sub_keys_2"].transpose(0, 3, 1, 2)
    sent["peer_u"] = a["peer_u_2"].reshape(DEPTH * EXPERTS, D)
    sent["peer_v"] = a["peer_v_2"].reshape(DEPTH * EXPERTS, D)
    sent.update(tables())
    nc = bacc.Bacc("TRN2", target_bir_lowering=False, num_devices=1)
    arrays, ins = {}, {}
    for name, v in sent.items():
        arrays[f"in_{name}"] = np.ascontiguousarray(v)
        ins[name] = nc.dram_tensor(f"in_{name}", v.shape, mybir.dt.from_np(v.dtype), kind="ExternalInput").ap()
    out = nc.dram_tensor("out_0", (1, SEQ, D), F32, kind="ExternalOutput").ap()
    build(nc, ins, out)
    return run(nc, [arrays], core_ids=[0]).results[0]["out_0"]
```

```python
import math
from contextlib import ExitStack

import numpy as np

import concourse.bass as bass
from concourse import mybir

F32 = mybir.dt.float32
F32R = mybir.dt.float32r
I32 = mybir.dt.int32
U32 = mybir.dt.uint32
ALU = mybir.AluOpType
ACT = mybir.ActivationFunctionType
AX = mybir.AxisListType

P = 128
D = 1024
SEQ = 256
NT = SEQ // P
KC = D // P
DEPTH = 2
HEADS, KV_HEADS, HD = 16, 4, 64
GROUP = HEADS // KV_HEADS
ROT = HD // 4
HALF = ROT // 2
THETA = 500000.0
WINDOW = 128
D_FF = 2816
FC = D_FF // P
EPS = 1e-6
NEG = -1e30

R = 4
COLS = 512
SLOTS_A = 36
Q_S, KV_S, CB_S, CC_S, CX_S, GA_S, GB_S = 0, 2, 3, 5, 7, 9, 11
CONVP_S, ATTNP_S, OUT_S, FFN_S, DOWN_S = 13, 15, 17, 19, 30
Q0, KV0, CB0, CC0, CX0, GA0, GB0 = 0, 1024, 1536, 2560, 3584, 4608, 5632
DOWN_PIECES = [(0, 8), (8, 8), (16, 6)]
HALVES = 2 * (SLOTS_A - FFN_S)

D_UNITS = 4 + 4 + 4 + 4 + 4 + FC
A_UNITS = 4 + 2 + 4 + 6 + 4 + 4 + 4 + 4
G_PRE, G_FFN, CONVW = 0, KC, 2 * KC
NCOL = 2 * KC + 3 * KC

LSTM_HEADS, LSTM_QK, LSTM_V, LSTM_CONV = 8, 64, 128, 4
SB_HEADS, SB_DIM = 16, 64
PEER_HEADS, NKEYS, TOPK = 8, 128, 16
EXPERTS = NKEYS * NKEYS
ADA_CHUNKS = 2 * 6 * KC + 2 * KC
ADA_LAYER = ADA_CHUNKS // DEPTH
KV_ADA = 2 * 6 * KC
PICKS = PEER_HEADS * TOPK
RING = 8
PAIR = 2 * TOPK
TURNS = PICKS // PAIR
PE_ROWS = 3 * TOPK
DIAGS = 8
PE_FIRST = [0] + [PICKS - PE_ROWS] * NT
S2 = DEPTH * SLOTS_A
N_MIX, N_FFN, N_KV, LCONV = 0, 2 * KC, 4 * KC, 5 * KC
NCOL2 = 5 * KC + LSTM_CONV * KC
PEER_A_UNITS = 4 + 8 + 8 + 2
LSTM_A_UNITS = 6 + 8 + LSTM_HEADS + 4
TILE_A_UNITS = 10 + 2 + 2 + 2 + 4 + 4
SLOTS_B, R2, SLOTS_T = 16, 2, 12
STICK_GROUPS = [[[h + p + 2 * i for i in range(4)] for h in (0, 8) for p in range(2)],
                [[h + p + 2 * i for i in range(2)] for h in (0, 4, 8, 12) for p in range(2)]]
STICK_BEFORE = [0, len(STICK_GROUPS[0])]
STICK_FULL = [DEPTH * A_UNITS + LSTM_A_UNITS + PEER_A_UNITS + TILE_A_UNITS * t + 11 for t in range(NT)]


def build(nc, ins, out):
    ctx = ExitStack()
    with ctx:
        def sem(name):
            return ctx.enter_context(nc.semaphore(name))

        def psum(name):
            return ctx.enter_context(nc.psum_tensor(name, [P, 512], F32))

        def sb(name, shape, dt=F32, stack=ctx):
            return stack.enter_context(nc.sbuf_tensor(name, shape, dt))

        ident = sb("ident", [P, P])
        x = sb("x", [P, NT, D])
        normed = ExitStack()
        xn = sb("xn", [P, NT, D], F32, normed)
        normed.close()
        flo_b = sb("flo_b", [P, KC, SEQ], F32R)
        hT = sb("hT", [P, KC, SEQ])
        wring = sb("wring", [P, R, KC, COLS])
        adac = sb("adac", [P, ADA_CHUNKS])
        adal = sb("adal", [P, ADA_LAYER])
        cols2 = sb("cols2", [P, NCOL2])
        adab = sb("adab", [P, ADA_CHUNKS])
        rsb = sb("rsb", [P, 32])
        modA = sb("modA", [P, 5, KC])
        cols = sb("cols", [P, NCOL])
        ssx = sb("ssx", [P, NT])
        rsx = sb("rsx", [P, NT])
        ssm = sb("ssm", [P, NT, 2])
        rsm = sb("rsm", [P, NT])
        junk = sb("junk", [P, D])
        rsv, rsa = sb("rsv", [P, 32]), sb("rsa", [P, 32])

        first = ExitStack()
        def sa(name, shape, dt=F32):
            return sb(name, shape, dt, first)
        post_gain = sa("rows", [P, 2, D])
        crow = sa("crow", [P, D])
        aring = sa("aring", [P, 2, D])
        mask8 = sa("mask8", [P, NT, SEQ])
        cs = sa("cs", [P, 2, NT, HALF])
        sinks = sa("sinks", [P, HEADS])
        silu = sa("silu", [P, 2, SEQ])
        att = ExitStack()
        def st(name, shape, dt=F32):
            return sb(name, shape, dt, att)
        cbT = st("cbT", [P, KC, SEQ])
        ccT = st("ccT", [P, KC, SEQ])
        uT = st("uT", [P, KC, SEQ + 2])
        cvt = st("cvt", [P, 2, SEQ])
        zrow = st("zrow", [P, NT, Q0 + CB0])
        kdup = st("kdup", [P, NT, KV_HEADS, 2, HD])
        qT = st("qT", [P, KC, SEQ])
        kT = st("kT", [P, KV_HEADS, SEQ])
        rt = st("rt", [P, 4, NT * (HEADS + KV_HEADS) * HALF])
        S = st("S", [P, 2, NT, SEQ])
        PR = st("PR", [P, 2, NT, SEQ])
        PT = st("PT", [P, 2, NT, SEQ])
        nm = st("nm", [P, HEADS, NT])
        rmx = st("rmx", [P, HEADS, NT])
        den = st("den", [P, HEADS, NT])
        es = st("es", [P, 4, NT])
        rden = st("rden", [P, NT, 4])
        sga = st("sga", [P, KC, SEQ])
        sgb = st("sgb", [P, KC, SEQ])
        att.close()
        whi = sa("whi", [P, 2, KC // 2, COLS], F32R)
        wlo = sa("wlo", [P, 2, KC // 2, COLS], F32R)
        hhi = sa("hhi", [P, KC, SEQ], F32R)
        hlo = sa("hlo", [P, KC, SEQ], F32R)
        fhi = sa("fhi", [P, FC, SEQ], F32R)
        flo_a = sa("flo_a", [P, FC - KC, SEQ], F32R)
        orow = xn
        oT = qT
        first.close()

        grows = sb("grows", [P, 3, D])
        lstm = ExitStack()
        def sl(name, shape, dt=F32):
            return sb(name, shape, dt, lstm)
        biglm = sl("biglm", [P, 3 * P])
        wg = sl("wg", [P, KC, 2 * LSTM_HEADS])
        bif = sl("bif", [LSTM_HEADS, 2])
        hng = sl("hng", [P, D])
        preT = sl("preT", [P, KC, SEQ + LSTM_CONV - 1])
        lcv = sl("lcv", [P, 2, SEQ])
        qkT = sl("qkT", [P, KC, SEQ])
        vaug = sl("vaug", [P, NT, LSTM_HEADS, LSTM_V + 1])
        so = sl("so", [P, NT, D])
        numS = sl("numS", [P, LSTM_HEADS, NT, LSTM_V + 1])
        gi, gf, ge, gl, gb_, gg, gM, gm, gone = [sl(n, [LSTM_HEADS, SEQ]) for n in
                                                 ("gi", "gf", "ge", "gl", "gb_", "gg", "gM", "gm", "gone")]
        gcol = sl("gcol", [P, 4, LSTM_HEADS])
        Dt = sl("Dt", [P, 2, 3 * P])
        Pl = sl("Pl", [P, 2, 3 * P])
        dcol = sl("dcol", [P, LSTM_HEADS, NT])
        rcol = sl("rcol", [P, LSTM_HEADS * NT])
        lstm.close()

        def se(name, shape, dt=F32):
            return sb(name, shape, dt)
        keysT = se("keysT", [P, 2, NKEYS])
        iota = se("iota", [P, TOPK])
        hrow = se("hrow", [P, NT, D])
        cand = se("cand", [P, PEER_HEADS, TOPK * TOPK])
        sc = se("sc", [P, 2 * PEER_HEADS, NKEYS])
        sc2 = se("sc2", [P, 2 * PEER_HEADS, NKEYS])
        top = se("top", [P, PEER_HEADS, 2, TOPK])
        topi = se("topi", [P, PEER_HEADS, 2, TOPK], U32)
        topf = se("topf", [P, PEER_HEADS, 2, TOPK])
        gt = se("gt", [P, PEER_HEADS, TOPK])
        pos = se("pos", [P, PEER_HEADS, TOPK], U32)
        hilo = se("hilo", [P, 2, PICKS], U32)
        hilof = se("hilof", [P, 2, PICKS])
        ef = se("ef", [P, 2, PICKS])
        eidx = se("eidx", [P, NT, PICKS + PAIR], I32)
        wsum = se("wsum", [P, PEER_HEADS])
        wexp = se("wexp", [P, NT, PEER_HEADS, TOPK])
        ix = se("ix", [P, 2, TOPK], I32)
        a16 = se("a16", [P, 2, TOPK])
        dots = se("dots", [P, PICKS])
        coef = se("coef", [P, PICKS])
        acc = junk
        gring = wring[:, R2:R].rearrange("p r k n -> p (r k n)").rearrange("p (r d) -> p r d", d=D)
        early = ExitStack()
        qp0 = sb("qp0", [P, NT, 2 * PEER_HEADS, P], F32, early)
        sc1 = sb("sc1", [P, 2 * PEER_HEADS, NKEYS], F32, early)
        early.close()
        qpt = cand[:, :, :].rearrange("p h (a n) -> p (h a) n", a=2)

        def sk(name, shape, dt=F32):
            return sb(name, shape, dt)
        before = sk("before", [P, P])
        tri = sk("tri", [P, P])
        ones = sk("ones", [P, P])
        qkg = sk("qkg", [P, 2, SB_DIM])
        hkT = sk("hkT", [P, KC, P])
        krow, qrow = sk("krow", [P, D]), sk("qrow", [P, D])
        vrow = sk("vrow", [P, NT, D])
        skT = sk("skT", [P, KC, SEQ])
        sqT = sk("sqT", [P, KC, P])
        srs, sss = sk("srs", [P, SB_HEADS]), sk("sss", [P, SB_HEADS])
        az, sp_, ls, ex = [sk(n, [P, 2, 512]) for n in ("az", "sp_", "ls", "ex")]

        diag = az[:, :, :].rearrange("p a n -> p (a n)").rearrange("p (r n) -> p r n", n=P)
        assert DIAGS * P == 2 * 512

        pd = [psum("pd0"), psum("pd1")]
        pa = [psum("pa0"), psum("pa1")]
        pr = [psum(f"pr{i}") for i in range(4)]
        psc, ppt, po = pr[0:2], pr[2], pr[3]

        w_in_slot = [sem(f"w_in_slot{i}") for i in range(R)]
        w_free = sem("w_free")
        x_in = sem("x_in")
        const_in = sem("const_in")
        par_in = sem("par_in")
        par_free = sem("par_free")
        pd_full, pd_free = sem("pd_full"), sem("pd_free")
        pa_full, pa_free = sem("pa_full"), sem("pa_free")
        x_ready = sem("x_ready")
        ss_ready = sem("ss_ready")
        xn_ready = sem("xn_ready")
        hT_ready = sem("hT_ready")
        rope_done = sem("rope_done")
        qk_ready = sem("qk_ready")
        sc_full, sc_seen, sc_read = sem("sc_full"), sem("sc_seen"), sem("sc_read")
        nm_ready, p_ready = sem("nm_ready"), sem("p_ready")
        pt_full, pt_ready = sem("pt_full"), sem("pt_ready")
        o_full, o_read = sem("o_full"), sem("o_read")
        o_used = sem("o_used")
        o_rows = sem("o_rows")
        es_sum, es_ready = sem("es_sum"), sem("es_ready")
        cc_ready = sem("cc_ready")
        sig_ready = sem("sig_ready")
        yconv_ready = sem("yconv_ready")
        mix_ready = sem("mix_ready")
        row_full, row_read = sem("row_full"), sem("row_read")
        ssm_ready = sem("ssm_ready")
        silu_ready, silu_free = sem("silu_ready"), sem("silu_free")
        f_ready = sem("f_ready")
        whi_ready, wlo_ready = sem("whi_ready"), sem("wlo_ready")
        even_half_used, down_half_used = sem("even_half_used"), sem("down_half_used")
        out_done = sem("out_done")
        c_in, c_ready = sem("c_in"), sem("c_ready")
        ada_in, ada_free, ada_ready = [sem("ada_in0"), sem("ada_in1")], sem("ada_free"), sem("ada_ready")
        cols2_in, lstm_in, stick_in, experts_in = sem("cols2_in"), sem("lstm_in"), sem("stick_in"), sem("experts_in")
        mod_ready = sem("mod_ready")
        grows_ready = sem("grows_ready")
        v_ready = sem("v_ready")
        qk_pre, qk_silu = sem("qk_pre"), sem("qk_silu")
        if_full, if_abs, if_log, if_sum, if_exp = sem("if_full"), sem("if_abs"), sem("if_log"), sem("if_sum"), sem("if_exp")
        gcol_full, gcol_ready = sem("gcol_full"), sem("gcol_ready")
        m_full, m_read, st_full, st_read = sem("m_full"), sem("m_read"), sem("st_full"), sem("st_read")
        d_pre, d_ready, pl_ready = sem("d_pre"), sem("d_ready"), sem("pl_ready")
        num_ready, y_rows = sem("num_ready"), sem("y_rows")
        yT_ready = sem("yT_ready")
        srow_ready, sqk_ready, sT_ready = sem("srow_ready"), sem("sqk_ready"), sem("sT_ready")
        z_full, z_read, sL_ready = sem("z_full"), sem("z_read"), sem("sL_ready")
        spm_ready, cum_full, cum_read = sem("spm_ready"), sem("cum_full"), sem("cum_read")
        sp_ready, ex_ready, a_exp, a_ready, a_used = sem("sp_ready"), sem("ex_ready"), sem("a_exp"), sem("a_ready"), sem("a_used")
        qp_ready, sc_ready, chosen = sem("qp_ready"), sem("sc_ready"), sem("chosen")
        g_arg, g_exp = sem("g_arg"), sem("g_exp")
        ix_ready, rows_free, wait_seen = sem("ix_ready"), sem("rows_free"), sem("wait_seen")
        w2_in, w2_free = [sem("w2_in0"), sem("w2_in1")], sem("w2_free")
        tss_ready, txn_ready, thT_ready = sem("tss_ready"), sem("txn_ready"), sem("thT_ready")
        mixed, experts_done, stick_done = sem("mixed"), sem("experts_done"), sem("stick_done")
        ty_rows, tyT_ready = sem("ty_rows"), sem("tyT_ready")
        row_in = [sem(f"row_in{i}") for i in range(RING)]
        dots_ready, gelu_ready = sem("dots_ready"), sem("gelu_ready")
        handed, diag_ready, sums_full = sem("handed"), sem("diag_ready"), sem("sums_full")

        wcol = {k: ins[k] for k in ("w_in", "w_attn_proj", "w_conv_proj", "w_out", "w_gate", "w_up", "w_down")}

        block = ctx.enter_context(nc.Block())

        def taken_in(tt, q):
            return RING + (2 * tt + 1) * PICKS + q + 1

        def slot(i):
            return wring[:, i % R]

        def half_piece(n):
            k0, k = DOWN_PIECES[(n - FC) // 2 % 3]
            return k0 + n % 2 * (KC // 2), (k - KC // 2 if n % 2 else KC // 2)

        def flo(u):
            return flo_a[:, u, :] if u < FC - KC else flo_b[:, u - (FC - KC), :]

        def raw_half(n):
            nk = KC // 2 if n < FC else half_piece(n)[1]
            at = (n % 2) * (KC // 2)
            return slot(FFN_S + n // 2)[:, at:at + nk, :], slice(0, nk)

        @block.sync
        def _(sp):
            sp.dma_start(crow[:, :], ins["c_2"].partition_broadcast(P).rearrange("p a n -> p (a n)")).then_inc(c_in, 16)
            sp.dma_start(x[:, :, :], ins["x"].rearrange("b (t p) d -> p (b t) d", p=P)).then_inc(x_in, 16)
            sp.dma_start(ident[:, :], ins["c_ident"]).then_inc(const_in, 16)
            sp.dma_start(mask8[:, :, :], ins["c_mask8"]).then_inc(const_in, 16)
            sp.dma_start(cs[:, :, :, :], ins["c_cs"]).then_inc(const_in, 16)

            def load(l, i, parts):
                sp.wait_ge(w_free, l * SLOTS_A + i + 1)
                for dst, src in parts:
                    sp.dma_start(dst, src).then_inc(w_in_slot[i % R], 16)

            def cut(w, l, c0, n, k0=0, k=KC):
                v = w[bass.ds(l, 1), k0 * P:(k0 + k) * P, c0:c0 + n]
                return v.rearrange("a (k p) n -> p (a k) n", p=P)

            def params(l):
                sp.wait_ge(par_free, 2 * l + 2)
                sp.dma_start(cols[:, :], ins["cols_a"][bass.ds(l, 1)].rearrange("a p n -> p (a n)")).then_inc(par_in, 16)
                sp.dma_start(sinks[:, :], ins["attn_sink"][bass.ds(l, 1), :].partition_broadcast(P).rearrange("p a h -> p (a h)")).then_inc(par_in, 16)
                sp.dma_start(post_gain[:, 0, :], ins["g_post_mix"][bass.ds(l, 1), :].partition_broadcast(P).rearrange("p a h -> p (a h)")).then_inc(par_in, 16)
                sp.dma_start(post_gain[:, 1, :], ins["g_post_ffn"][bass.ds(l, 1), :].partition_broadcast(P).rearrange("p a h -> p (a h)")).then_inc(par_in, 16)

            sp.dma_start(cols2[:, :], ins["cols_b"]).then_inc(cols2_in, 16)
            sp.dma_start(adab[:, :], ins["ada_bias"]).then_inc(cols2_in, 16)
            with sp.Fori(0, DEPTH) as l:
                for i in range(SLOTS_A):
                    if i == 1:
                        params(l)
                    if i < CONVP_S:
                        parts = [(slot(i), cut(ins["w_in"], l, i * COLS, COLS))]
                    elif i < FFN_S:
                        w, s0 = {0: ("w_conv_proj", CONVP_S), 1: ("w_attn_proj", ATTNP_S), 2: ("w_out", OUT_S)}[(i - CONVP_S) // 2]
                        parts = [(slot(i), cut(ins[w], l, (i - s0) * COLS, COLS))]
                    elif i < DOWN_S:
                        c0 = (i - FFN_S) * 256
                        parts = [(slot(i)[:, :, 0:256], cut(ins["w_gate"], l, c0, 256)),
                                 (slot(i)[:, :, 256:512], cut(ins["w_up"], l, c0, 256))]
                    else:
                        h, (k0, k) = (i - DOWN_S) // 3, DOWN_PIECES[(i - DOWN_S) % 3]
                        parts = [(slot(i)[:, 0:k, :], cut(ins["w_down"], l, h * COLS, COLS, k0, k))]
                    load(l, i, parts)
            def small_lstm():
                sp.wait_ge(x_ready, 2 * DEPTH + 1)
                sp.dma_start(biglm[:, :], ins["c_biglm"]).then_inc(lstm_in, 16)
                sp.dma_start(wg[:, :, :], ins["ma_w_in_2"][0, :, 6 * COLS:6 * COLS + 16].rearrange("(k p) n -> p k n", p=P)).then_inc(lstm_in, 16)
                sp.dma_start(bif[:, :], ins["b_if"]).then_inc(lstm_in, 16)
                sp.dma_start(hng[:, :], ins["hnorm"].partition_broadcast(P).rearrange("p a n -> p (a n)")).then_inc(lstm_in, 16)

            def cols_of(name, n, l=0):
                w = ins[name]
                w = w[l] if len(w.shape) == 3 else w
                return [w[:, c * COLS:(c + 1) * COLS].rearrange("(k p) n -> p k n", p=P) for c in range(n)]

            for j, src in enumerate(cols_of("ma_w_in_2", 6) + cols_of("ma_w_out_2", 2) + 2 * cols_of("peer_w_q_2", 4)):
                if j == R:
                    small_lstm()
                if j == SLOTS_B - 4:
                    sp.wait_ge(mixed, 1)
                    sp.dma_start(keysT[:, :, :], ins["keysT"][0]).then_inc(experts_in, 16)
                    sp.dma_start(iota[:, :], ins["c_iota"]).then_inc(experts_in, 16)
                sp.wait_ge(w_free, S2 + j + 1)
                sp.dma_start(slot(j), src).then_inc(w_in_slot[j % R], 16)
            sp.wait_ge(w_free, S2 + SLOTS_B + R)
            per_tile = (cols_of("kv_w_2", 4) + cols_of("sb_w_q_2", 2) + cols_of("sb_w_out_2", 2) + cols_of("peer_w_q_2", 4, 1))
            for m in range(NT * SLOTS_T):
                if m == R2:
                    sp.wait_ge(chosen, NT)
                    sp.dma_start(before[:, :], ins["c_before"]).then_inc(stick_in, 16)
                    sp.dma_start(tri[:, :], ins["c_tri"]).then_inc(stick_in, 16)
                    sp.dma_start(ones[:, :], ins["c_ones"]).then_inc(stick_in, 16)
                    sp.dma_start(qkg[:, 0, :], ins["k_norm_g_2"].rearrange("(a n) -> a n", a=1).partition_broadcast(P).rearrange("p a n -> p (a n)")).then_inc(stick_in, 16)
                    sp.dma_start(qkg[:, 1, :], ins["sb_q_norm_g_2"].partition_broadcast(P).rearrange("p a n -> p (a n)")).then_inc(stick_in, 16)
                    sp.dma_start(keysT[:, :, :], ins["keysT"][1]).then_inc(stick_in, 16)
                if m >= R2:
                    sp.wait_ge(w2_free, m - R2 + 1)
                sp.dma_start(wring[:, m % R2], per_tile[m % SLOTS_T]).then_inc(w2_in[m % R2], 16)
            sp.wait_ge(experts_done, DEPTH * NT)
            sp.dma_start(out.rearrange("b (t p) d -> p (b t) d", p=P), x[:, :, :]).then_inc(out_done, 16)
            sp.wait_ge(out_done, 16)

        def landed(i):
            n = 0
            for j in range(i + 1):
                if j % R == i % R:
                    n += 32 if FFN_S <= j < DOWN_S else 16
            return n
        LANDED_LAYER = [landed(SLOTS_A - R + r) for r in range(R)]

        @block.tensor
        def _(pe):
            pe.sem_inc(w_free, R)
            pe.wait_ge(const_in, 48)

            def transposes(u, base, src, dst_full):
                ring, full, free = base
                pe.wait_ge(free, u + 1)
                return [nc.tensor.transpose(ring[:, i * P:(i + 1) * P], src(i), ident[:, :]) for i in range(4)][-1].then_inc(full, 1)

            def weights(l, i):
                pe.wait_ge(w_in_slot[i % R], l * LANDED_LAYER[i % R] + landed(i))

            with pe.Fori(0, DEPTH) as l:
                nd, na, owed = [0], [0], [0]

                def used_up():
                    owed[0] += 1

                def mm(out_, lhsT, rhs, start, stop):
                    m = nc.tensor.matmul(out_, lhsT, rhs, start=start, stop=stop)
                    if owed[0] and not stop:
                        m.then_inc(w_free, 1)
                        owed[0] -= 1
                    return m

                def bank_d():
                    u = nd[0]
                    nd[0] += 1
                    pe.wait_ge(pd_free, l * D_UNITS + u + 1)
                    return pd[u % 2]

                def bank_a():
                    u = na[0]
                    na[0] += 1
                    pe.wait_ge(pa_free, l * A_UNITS + u + 1)
                    return pa[u % 2]

                def norm_transposes(n):
                    pe.wait_ge(xn_ready, 2 * l + n + 1)
                    for j in range(KC // 2):
                        b = bank_d()
                        for i in range(4):
                            c, t = 2 * j + i // 2, i % 2
                            m = nc.tensor.transpose(b[:, i * P:(i + 1) * P], xn[:, t, c * P:(c + 1) * P], ident[:, :])
                        m.then_inc(pd_full, 1)

                def row_unit(b, i, t, full, release):
                    for k in range(KC):
                        m = mm(b[:, :], hT[:, k, t * P:(t + 1) * P], slot(i)[:, k, :],
                                             start=(k == 0), stop=(k == KC - 1))
                    m.then_inc(full, 1)
                    if release:
                        used_up()

                def col_unit(b, i, half, src, full, release):
                    for c in range(2):
                        for k in range(KC):
                            m = mm(b[:, c * SEQ:(c + 1) * SEQ], slot(i)[:, k, (2 * half + c) * P:(2 * half + c + 1) * P],
                                                 src[:, k, :], start=(k == 0), stop=(k == KC - 1))
                    m.then_inc(full, 1)
                    if release:
                        used_up()

                norm_transposes(0)
                pe.wait_ge(hT_ready, 2 * l + 1)
                for i in (Q_S, Q_S + 1, KV_S):
                    weights(l, i)
                    for t in range(NT):
                        row_unit(bank_a(), i, t, pa_full, t == 1)
                for i in (CB_S, CB_S + 1):
                    weights(l, i)
                    for half in range(2):
                        col_unit(bank_a(), i, half, hT, pa_full, half == 1)
                pe.wait_ge(rope_done, l + 1)
                for j in range(KC // 2):
                    b = bank_a()
                    for i in range(4):
                        c, t = 2 * j + i // 2, i % 2
                        m = nc.tensor.transpose(b[:, i * P:(i + 1) * P], zrow[:, t, c * P:(c + 1) * P], ident[:, :])
                    m.then_inc(pa_full, 1)
                for j in range(KV_HEADS // 2):
                    b = bank_a()
                    for i in range(4):
                        g, t = 2 * j + i // 2, i % 2
                        m = nc.tensor.transpose(b[:, i * P:(i + 1) * P], kdup[:, t, g].rearrange("p a d -> p (a d)"), ident[:, :])
                    m.then_inc(pa_full, 1)

                def scores(h):
                    if h == 0:
                        pe.wait_ge(qk_ready, l + 1)
                    pe.wait_ge(sc_read, l * HEADS + h + 1)
                    b0 = (h % 2) * HD
                    for t in range(NT):
                        m = mm(psc[h % 2][:, t * SEQ:(t + 1) * SEQ], qT[b0:b0 + HD, h // 2, t * P:(t + 1) * P],
                                             kT[b0:b0 + HD, h // GROUP, :], start=True, stop=True)
                    m.then_inc(sc_full, 1)

                def prob_transposes(h):
                    pe.wait_ge(p_ready, l * HEADS + h + 1)
                    pe.wait_ge(pt_ready, l * HEADS + h + 1)
                    for i in range(4):
                        t, c = i // 2, i % 2
                        m = nc.tensor.transpose(ppt[:, i * P:(i + 1) * P], PR[:, h % 2, t, c * P:(c + 1) * P], ident[:, :])
                    m.then_inc(pt_full, 1)

                def values(h):
                    pe.wait_ge(pt_ready, l * HEADS + h + 2)
                    if h % 4 == 0:
                        pe.wait_ge(o_read, l * (HEADS // 4) + h // 4 + 1)
                    for t in range(NT):
                        o = po[:, (t * 4 + h % 4) * HD:(t * 4 + h % 4 + 1) * HD]
                        v0 = Q0 + KV0_V + (h // GROUP) * HD
                        for c in range(NT):
                            m = mm(o, PT[:, h % 2, t, c * P:(c + 1) * P], zrow[:, c, v0:v0 + HD],
                                                 start=(c == 0), stop=(c == 1))
                    m.then_inc(o_full, 1)

                KV0_V = 1024 + KV_HEADS * HD
                for s in range(16):
                    i = CC_S + s // 2
                    if s % 2 == 0:
                        weights(l, i)
                    if CX_S <= i < GA_S:
                        col_unit(bank_d(), i, s % 2, hT, pd_full, s % 2 == 1)
                    else:
                        col_unit(bank_a(), i, s % 2, hT, pa_full, s % 2 == 1)
                    if s >= 2:
                        values(s - 2)
                    if s >= 1:
                        prob_transposes(s - 1)
                    scores(s)
                for s in range(4):
                    i = CONVP_S + s // 2
                    if s % 2 == 0:
                        weights(l, i)
                    if s == 0:
                        pe.wait_ge(yconv_ready, l + 1)
                    col_unit(bank_d(), i, s % 2, cbT, pd_full, s % 2 == 1)
                    if s == 0:
                        values(HEADS - 2)
                        prob_transposes(HEADS - 1)
                    if s == 1:
                        values(HEADS - 1)
                pe.wait_ge(o_rows, (l + 1) * (HEADS // 4))
                for j in range(KC // 2):
                    b = bank_a()
                    for i in range(4):
                        c, t = 2 * j + i // 2, i % 2
                        m = nc.tensor.transpose(b[:, i * P:(i + 1) * P], orow[:, t, c * P:(c + 1) * P], ident[:, :])
                    m.then_inc(pa_full, 1)
                for s in range(4):
                    i = ATTNP_S + s // 2
                    if s % 2 == 0:
                        weights(l, i)
                    if s == 0:
                        pe.wait_ge(o_used, l + 1)
                    col_unit(bank_d(), i, s % 2, oT, pd_full, s % 2 == 1)

                def row_outputs():
                    for half in range(2):
                        i = OUT_S + half
                        weights(l, i)
                        for t in range(NT):
                            pe.wait_ge(row_read, 4 * (2 * l) + 2 * half + t + 1)
                            for k in range(KC):
                                m = mm(pr[2 * t + half][:, :], sga[:, k, t * P:(t + 1) * P], slot(i)[:, k, :],
                                       start=(k == 0), stop=(k == KC - 1))
                            m.then_inc(row_full, 1)
                        used_up()

                def split_row_outputs():
                    for n in range(FC, HALVES):
                        i, (half, piece) = FFN_S + n // 2, divmod((n - FC) // 2, 3)
                        k0, nk = half_piece(n)
                        pe.wait_ge(wlo_ready, l * HALVES + n + 1)
                        if n % 2:
                            used_up()
                        for t in range(NT):
                            if k0 == 0:
                                pe.wait_ge(row_read, 4 * (2 * l + 1) + 2 * half + t + 1)
                            cut = slice(t * P, (t + 1) * P)
                            for k in range(nk):
                                for q, (f, w) in enumerate(((fhi[:, k0 + k, cut], whi), (fhi[:, k0 + k, cut], wlo), (flo(k0 + k)[:, cut], whi))):
                                    last = k0 + k == FC - 1 and q == 2
                                    m = mm(pr[2 * t + half][:, :], f, w[:, n % 2, k, :],
                                           start=(k0 + k == 0 and q == 0), stop=last)
                            if last:
                                m.then_inc(row_full, 1)
                        pe.drain().then_inc(down_half_used, 1)

                pe.wait_ge(mix_ready, l + 1)
                row_outputs()
                norm_transposes(1)
                pe.wait_ge(hT_ready, 2 * l + 2)
                def split_products(b, half, c):
                    for g in range(2):
                        at = g * 256 + c * P
                        for k in range(KC // 2):
                            kk = half * (KC // 2) + k
                            for n, (w, h) in enumerate(((whi, hhi), (whi, hlo), (wlo, hhi))):
                                m = mm(b[:, g * SEQ:(g + 1) * SEQ], w[:, half, k, at:at + P], h[:, kk, :],
                                       start=(g == 0 and kk == 0 and n == 0), stop=(g == 1 and kk == KC - 1 and n == 2))
                    return m

                for i in range(FFN_S, DOWN_S):
                    banks = []
                    for half in range(2):
                        pe.wait_ge(wlo_ready, l * HALVES + 2 * (i - FFN_S) + half + 1)
                        if half:
                            used_up()
                        for c in range(2):
                            if half == 0:
                                banks.append(bank_d())
                            m = split_products(banks[c], half, c)
                            if half:
                                m.then_inc(pd_full, 1)
                        if half == 0:
                            assert owed[0] == 0
                            m.then_inc(even_half_used, 1)
                pe.wait_ge(f_ready, l + 1)
                split_row_outputs()
                assert owed[0] == 0
                assert (nd[0], na[0]) == (D_UNITS, A_UNITS)

            nd, na, owed = [DEPTH * D_UNITS], [DEPTH * A_UNITS], [0]

            def bank_d():
                u = nd[0]
                nd[0] += 1
                pe.wait_ge(pd_free, u + 1)
                return pd[u % 2]

            def bank_a():
                u = na[0]
                na[0] += 1
                pe.wait_ge(pa_free, u + 1)
                return pa[u % 2]

            def mm(out_, lhsT, rhs, start, stop):
                m = nc.tensor.matmul(out_, lhsT, rhs, start=start, stop=stop)
                if owed[0] and not stop:
                    m.then_inc(w_free, 1)
                    owed[0] -= 1
                return m

            def weights(j):
                pe.wait_ge(w_in_slot[j % R], DEPTH * LANDED_LAYER[j % R] + 16 * (j // R + 1))

            def row_unit(b, j, t, src, full):
                for k in range(KC):
                    m = mm(b[:, :], src[:, k, t * P:(t + 1) * P], slot(j)[:, k, :], k == 0, k == KC - 1)
                m.then_inc(full, 1)
                owed[0] += t

            def col_unit(b, j, half, src, full):
                for c in range(2):
                    for k in range(KC):
                        m = mm(b[:, c * SEQ:(c + 1) * SEQ], slot(j)[:, k, (2 * half + c) * P:(2 * half + c + 1) * P],
                               src[:, k, :], k == 0, k == KC - 1)
                m.then_inc(full, 1)
                owed[0] += half

            def to_columns(src, bank, full):
                for j in range(KC // 2):
                    b = bank()
                    for i in range(4):
                        c, t = 2 * j + i // 2, i % 2
                        m = nc.tensor.transpose(b[:, i * P:(i + 1) * P], src[:, t, c * P:(c + 1) * P], ident[:, :])
                    m.then_inc(full, 1)

            def tile_columns(bank, full, src):
                for half in range(2):
                    b = bank()
                    for i in range(4):
                        c = 4 * half + i
                        m = nc.tensor.transpose(b[:, i * P:(i + 1) * P], src[:, c * P:(c + 1) * P], ident[:, :])
                    m.then_inc(full, 1)

            def gate_row(c0):
                for half in range(2):
                    b = bank_a()
                    for i in range(4):
                        c = c0 + 4 * half + i
                        m = nc.tensor.matmul(b[:, i * P:(i + 1) * P], adac[:, c:c + 1].to_broadcast([P, P]), ident[:, :],
                                             start=True, stop=True)
                    m.then_inc(pa_full, 1)

            def gate_rows():
                pe.wait_ge(mod_ready, 1)
                for c0 in (2 * KC, 5 * KC, 11 * KC):
                    gate_row(c0)

            def experts_first():
                def columns_of_tile(t):
                    pe.wait_ge(txn_ready, t + 1)
                    tile_columns(bank_d, pd_full, xn[:, t])

                def queries(t, js):
                    for j in js:
                        m = NT * 4 + t * 4 + j
                        weights(m)
                        b = bank_a()
                        for c in range(4):
                            for k in range(KC):
                                i = mm(b[:, c * P:(c + 1) * P], slot(m)[:, k, c * P:(c + 1) * P], hT[:, k, t * P:(t + 1) * P],
                                       k == 0, k == KC - 1)
                        i.then_inc(pa_full, 1)
                        owed[0] += 1

                columns_of_tile(0)
                pe.wait_ge(thT_ready, 1)
                rows_back(0)
                queries(0, (0, 1))
                columns_of_tile(1)
                queries(0, (2, 3))
                pe.wait_ge(experts_in, 32)
                for t in range(NT):
                    if t:
                        pe.wait_ge(thT_ready, t + 1)
                        rows_back(t)
                        queries(t, range(4))
                    pe.wait_ge(qp_ready, t + 1)
                    key_scores(lambda hp: qp0[:, t, hp, :])
                pe.drain().then_inc(w_free, 1)
                owed[0] = 0
                gate_row(8 * KC)

            def rows_back(t):
                for half in range(2):
                    b = bank_a()
                    for i in range(4):
                        m = nc.tensor.transpose(b[:, i * P:(i + 1) * P], hT[:, 4 * half + i, t * P:(t + 1) * P], ident[:, :])
                    m.then_inc(pa_full, 1)

            def key_scores(q):
                for q4 in range(4):
                    b = bank_a()
                    for i in range(4):
                        hp = 4 * q4 + i
                        m = nc.tensor.matmul(b[:, i * P:(i + 1) * P], q(hp), keysT[:, hp % 2, :], start=True, stop=True)
                    m.then_inc(pa_full, 1)

            gate_rows()
            pe.wait_ge(xn_ready, 2 * DEPTH + 1)
            to_columns(xn, bank_d, pd_full)
            pe.wait_ge(hT_ready, 2 * DEPTH + 1)
            for s in range(4):
                if s % 2 == 0:
                    weights(s // 2)
                col_unit(bank_d(), s // 2, s % 2, hT, pd_full)
            pe.wait_ge(lstm_in, 64)
            for g in range(2):
                for k in range(KC):
                    m = mm(pr[0][0:LSTM_HEADS, g * SEQ:(g + 1) * SEQ], wg[:, k, g * LSTM_HEADS:(g + 1) * LSTM_HEADS], hT[:, k, :],
                           k == 0, k == KC - 1)
            m.then_inc(if_full, 1)
            for j in range(2, 6):
                weights(j)
                for t in range(NT):
                    row_unit(bank_a(), j, t, hT, pa_full)
            pe.wait_ge(if_exp, 1)
            for i in range(4):
                src = (gg, gm)[i // 2]
                m = nc.tensor.transpose(pr[1][:, i * LSTM_HEADS:(i + 1) * LSTM_HEADS], src[:, (i % 2) * P:(i % 2 + 1) * P],
                                        ident[0:LSTM_HEADS, 0:LSTM_HEADS])
            m.then_inc(gcol_full, 1)
            pe.wait_ge(gcol_ready, 1)
            pe.wait_ge(qk_silu, KC // 2)
            pe.wait_ge(v_ready, 1)

            def lstm_scores(h):
                b0 = (h % 2) * LSTM_QK
                if h >= 2:
                    pe.wait_ge(m_read, h - 1)
                nc.tensor.matmul(pr[h % 2][:, 0:SEQ], ident[0:LSTM_HEADS, h:h + 1].to_broadcast([LSTM_HEADS, P]), gM[:, :],
                                 start=True, stop=True).then_inc(m_full, 1)
                if h >= 2:
                    pe.wait_ge(st_read, h - 1)
                k_, q_ = qkT[b0:b0 + LSTM_QK, KC // 2 + h // 2, :], qkT[b0:b0 + LSTM_QK, h // 2, :]
                nc.tensor.matmul(pr[2 + h % 2][:, 0:SEQ], k_[:, 0:P], q_, start=True, stop=True)
                nc.tensor.matmul(pr[2 + h % 2][:, SEQ:3 * P], k_[:, P:SEQ], q_[:, P:SEQ], start=True, stop=True).then_inc(st_full, 1)

            def lstm_values(h):
                pe.wait_ge(pl_ready, h + 1)
                b = bank_a()
                n = LSTM_V + 1
                nc.tensor.matmul(b[:, 0:n], Pl[:, h % 2, 0:P], vaug[:, 0, h, :], start=True, stop=True)
                nc.tensor.matmul(b[:, n:2 * n], Pl[:, h % 2, P:2 * P], vaug[:, 0, h, :], start=True, stop=False)
                nc.tensor.matmul(b[:, n:2 * n], Pl[:, h % 2, 2 * P:3 * P], vaug[:, 1, h, :], start=False, stop=True).then_inc(pa_full, 1)

            for h in range(LSTM_HEADS + 1):
                if h < LSTM_HEADS:
                    lstm_scores(h)
                if h:
                    lstm_values(h - 1)
            pe.wait_ge(y_rows, 1)
            to_columns(xn, bank_a, pa_full)
            pe.wait_ge(yT_ready, 1)
            for t in range(NT):
                for j in (6, 7):
                    weights(j)
                    row_unit(bank_d(), j, t, hT, pd_full)
            experts_first()

            def weighted_rows(tt):
                pe.wait_ge(handed, tt + 1)
                for i in range(PE_ROWS):
                    q = PE_FIRST[tt] + i
                    pe.wait_ge(row_in[q % RING], 16 * (PICKS // RING * (2 * tt + 1) + q // RING + 1))
                    pe.wait_ge(diag_ready, PE_ROWS * tt + i + 1)
                    for half in range(2):
                        m = nc.tensor.matmul(pr[half][:, :], diag[:, i % DIAGS, :], gring[:, q % RING, half * 512:(half + 1) * 512],
                                             start=(i == 0), stop=(i == PE_ROWS - 1))
                    m.then_inc(rows_free, 1)
                pe.drain().then_inc(sums_full, 1)

            def weights2(m):
                pe.wait_ge(w2_in[m % R2], 16 * (m // R2 + 1))

            def used2():
                pe.drain().then_inc(w2_free, 1)

            def tile_rows(bank, full, m, src):
                weights2(m)
                b = bank()
                for k in range(KC):
                    i = nc.tensor.matmul(b[:, :], src(k), wring[:, m % R2, k, :], start=(k == 0), stop=(k == KC - 1))
                i.then_inc(full, 1)
                used2()

            def second_layer(t):
                m0, cut = t * SLOTS_T, slice(t * P, (t + 1) * P)
                pe.wait_ge(txn_ready, NT + 2 * t + 1)
                tile_columns(bank_d, pd_full, xn[:, t])
                pe.wait_ge(thT_ready, NT + 2 * t + 1)
                for j in range(6):
                    src = hkT[:, :, :] if j < 4 else hT[:, :, cut]
                    tile_rows(bank_a, pa_full, m0 + j, lambda k: src[:, k, :])
                pe.wait_ge(sqk_ready, 2 * t + 1)
                tile_columns(bank_a, pa_full, krow)
                pe.wait_ge(sqk_ready, 2 * t + 2)
                tile_columns(bank_a, pa_full, qrow)
                pe.wait_ge(sT_ready, t + 1)
                pe.wait_ge(stick_in, 96)
                groups, g0, ks = STICK_GROUPS[t], STICK_BEFORE[t], t + 1

                def z_scores(g):
                    n = g0 + g
                    if n >= 2:
                        pe.wait_ge(z_read, n - 1)
                    for i, h in enumerate(groups[g]):
                        b0 = (h % 2) * SB_DIM
                        for s in range(ks):
                            at = (i * ks + s) * P
                            m = nc.tensor.matmul(pr[n % 2][:, at:at + P], skT[b0:b0 + SB_DIM, h // 2, s * P:(s + 1) * P],
                                                 sqT[b0:b0 + SB_DIM, h // 2, :], start=True, stop=True)
                    m.then_inc(z_full, 1)

                def sums_after(g):
                    n = g0 + g
                    pe.wait_ge(spm_ready, n + 1)
                    if n >= 2:
                        pe.wait_ge(cum_read, n - 1)
                    b, v = pr[2 + n % 2], sp_[:, n % 2, :]
                    m = nc.tensor.matmul(b[:, :], tri[:, :], v, start=True, stop=(t == 0))
                    if t:
                        m = nc.tensor.matmul(b[:, :].rearrange("p (i s n) -> p i s n", s=2, n=P)[:, :, 0, :], ones[:, :],
                                             v.rearrange("p (i s n) -> p i s n", s=2, n=P)[:, :, 1, :], start=False, stop=True)
                    m.then_inc(cum_full, 1)

                held = []

                def stick_values(g):
                    n = g0 + g
                    if g == 0:
                        held.extend([bank_a(), bank_a()])
                    pe.wait_ge(a_ready, n + 1)
                    for i, h in enumerate(groups[g]):
                        c = slice((h % 8) * SB_DIM, (h % 8 + 1) * SB_DIM)
                        for s in range(ks):
                            at = (i * ks + s) * P
                            m = nc.tensor.matmul(held[h // 8][:, c], ex[:, n % 2, at:at + P], vrow[:, s, h * SB_DIM:(h + 1) * SB_DIM],
                                                 start=(s == 0), stop=(s == ks - 1))
                    m.then_inc(pa_full if g in (len(groups) // 2 - 1, len(groups) - 1) else a_used, 1)

                for g in range(len(groups) + 2):
                    if g < len(groups):
                        z_scores(g)
                    if 1 <= g <= len(groups):
                        sums_after(g - 1)
                    if g >= 2:
                        stick_values(g - 2)
                pe.wait_ge(ty_rows, t + 1)
                tile_columns(bank_a, pa_full, xn[:, t])
                pe.wait_ge(tyT_ready, t + 1)
                for j in (6, 7):
                    tile_rows(bank_d, pd_full, m0 + j, lambda k: hT[:, k, cut])
                pe.wait_ge(txn_ready, NT + 2 * t + 2)
                tile_columns(bank_d, pd_full, xn[:, t])
                pe.wait_ge(thT_ready, NT + 2 * t + 2)
                rows_back(t)
                for j in range(8, 12):
                    m = m0 + j
                    weights2(m)
                    b = bank_a()
                    for c in range(4):
                        for k in range(KC):
                            i = nc.tensor.matmul(b[:, c * P:(c + 1) * P], wring[:, m % R2, k, c * P:(c + 1) * P], hT[:, k, cut],
                                                 start=(k == 0), stop=(k == KC - 1))
                    i.then_inc(pa_full, 1)
                    used2()
                pe.wait_ge(qp_ready, NT + t + 1)
                key_scores(lambda hp: qpt[:, hp, :])
                weighted_rows(1 + t)

            weighted_rows(0)
            for t in range(NT):
                second_layer(t)

        @block.scalar
        def _(act):
            act.sem_inc(pa_free, 2)
            act.wait_ge(c_in, 16)
            nc.scalar.activation(crow[:, :], crow[:, :], ACT.Silu).then_inc(c_ready, 1)
            act.wait_ge(x_in, 16)

            with act.Fori(0, DEPTH) as l:
                na = [0]

                def take():
                    u = na[0]
                    na[0] += 1
                    act.wait_ge(pa_full, l * A_UNITS + u + 1)
                    return pa[u % 2][:, :]

                def squares(n):
                    act.wait_ge(x_ready, 2 * l + n + 1)
                    for t in range(NT):
                        if t:
                            act.drain()
                        m = nc.scalar.activation(junk[:, :], x[:, t, :], ACT.Square, accum_out=ssx[:, t:t + 1])
                    m.then_inc(ss_ready, 1)
                    act.drain()

                def row_squares(n):
                    for half in range(2):
                        for t in range(NT):
                            act.wait_ge(row_full, 4 * (2 * l + n) + 2 * half + t + 1)
                            nc.scalar.activation(junk[:, (half) * 512:(half + 1) * 512], pr[2 * t + half][:, :], ACT.Square,
                                                 accum_out=ssm[:, t, half:half + 1]).then_inc(ssm_ready, 1)
                            act.drain()

                squares(0)
                for s in range(3):
                    for t in range(NT):
                        m = nc.scalar.copy(zrow[:, t, s * 512:(s + 1) * 512], take()).then_inc(pa_free, 1)
                act.drain()
                act.sem_inc(qk_ready, 1)
                for j in range(4):
                    nc.scalar.copy(cbT[:, 2 * j:2 * j + 2, :].rearrange("p c n -> p (c n)"), take()).then_inc(pa_free, 1)
                for j in range(4):
                    nc.scalar.copy(qT[:, 2 * j:2 * j + 2, :].rearrange("p c n -> p (c n)"), take()).then_inc(pa_free, 1)
                for j in range(2):
                    nc.scalar.copy(kT[:, 2 * j:2 * j + 2, :].rearrange("p c n -> p (c n)"), take()).then_inc(pa_free, 1)
                act.drain()
                act.sem_inc(qk_ready, 1)
                for s in range(16):
                    i = CC_S + s // 2
                    j = s % 4
                    dst = {0: ccT, 2: sga, 3: sgb}.get(s // 4)
                    if dst is not None:
                        func = ACT.Copy if dst is ccT else ACT.Sigmoid
                        d = dst[:, 2 * j:2 * j + 2, :].rearrange("p c n -> p (c n)")
                        nc.scalar.activation(d, take(), func).then_inc(pa_free, 1)
                        if dst is ccT:
                            act.drain()
                            act.sem_inc(cc_ready, 1)
                    for t in range(NT):
                        act.wait_ge(nm_ready, l * HEADS + s + 1)
                        nc.scalar.activation(PR[:, s % 2, t, :], S[:, s % 2, t, :], ACT.Exp, bias=nm[:, s, t:t + 1],
                                             accum_out=den[:, s, t:t + 1])
                    act.drain()
                    act.sem_inc(p_ready, 1)
                    if s % 4 == 3:
                        act.wait_ge(es_sum, l * 4 + s // 4 + 1)
                        nc.scalar.activation(es[:, :, :], es[:, :, :], ACT.Exp).then_inc(es_ready, 1)
                act.sem_inc(sig_ready, 1)
                for j in range(4):
                    nc.scalar.copy(oT[:, 2 * j:2 * j + 2, :].rearrange("p c n -> p (c n)"), take()).then_inc(pa_free, 1)
                act.drain()
                act.sem_inc(o_used, 1)

                def upper_parts(h):
                    i = FFN_S + h // 2
                    if h % 2 == 0:
                        act.wait_ge(w_in_slot[i % R], l * LANDED_LAYER[i % R] + landed(i))
                    if h >= FC + 2:
                        act.wait_ge(down_half_used, l * (HALVES - FC) + h - FC - 1)
                    elif h >= 2 and h % 2 == 0:
                        act.wait_ge(even_half_used, l * (FC // 2) + h // 2)
                    raw, ks = raw_half(h)
                    nc.scalar.copy(whi[:, h % 2, ks, :], raw).then_inc(whi_ready, 1)

                act.wait_ge(mix_ready, l + 1)
                upper_parts(0)
                upper_parts(1)
                row_squares(0)
                squares(1)
                for u in range(FC):
                    if u % 2 == 0:
                        upper_parts(u + 2)
                    act.wait_ge(pd_full, l * D_UNITS + 20 + u + 1)
                    act.wait_ge(silu_free, l * FC + u + 1)
                    nc.scalar.activation(silu[:, u % 2, :], pd[u % 2][:, 0:SEQ], ACT.Silu).then_inc(silu_ready, 1)
                    if u % 2:
                        upper_parts(u + 2)
                for h in range(FC + 2, HALVES):
                    upper_parts(h)
                row_squares(1)
                assert na[0] == A_UNITS

            na = [DEPTH * A_UNITS]

            def take():
                u = na[0]
                na[0] += 1
                act.wait_ge(pa_full, u + 1)
                return pa[u % 2][:, :]

            def squares(n):
                act.wait_ge(x_ready, 2 * DEPTH + 1 + n)
                for t in range(NT):
                    if t:
                        act.drain()
                    m = nc.scalar.activation(junk[:, :], x[:, t, :], ACT.Square, accum_out=ssx[:, t:t + 1])
                m.then_inc(ss_ready, 1)
                act.drain()

            def flat(v):
                return v.rearrange("p c n -> p (c n)")

            def columns_out(dst, ready):
                for j in range(KC // 2):
                    nc.scalar.copy(flat(dst[:, 2 * j:2 * j + 2, :]), take()).then_inc(pa_free, 1)
                act.drain().then_inc(ready, 1)

            def experts_first():
                tile_squares(0, mixed)
                rows_back(0)
                for t in range(NT):
                    if t:
                        rows_back(t)
                    for j in range(4):
                        if (t, j) == (0, 1):
                            tile_squares(1, mixed)
                        nc.scalar.copy(flat(qp0[:, t, 4 * j:4 * j + 4, :]), take()).then_inc(pa_free, 1)
                    act.drain().then_inc(qp_ready, 1)
                    for q4 in range(4):
                        nc.scalar.copy(flat((sc, sc1)[t][:, 4 * q4:4 * q4 + 4, :]), take()).then_inc(pa_free, 1)
                    act.drain().then_inc(sc_ready, 1)
                for half in range(2):
                    nc.scalar.copy(grows[:, 0, half * 512:(half + 1) * 512], take()).then_inc(pa_free, 1)

            def tile_squares(t, done):
                act.wait_ge(done, t + 1)
                nc.scalar.activation(xn[:, t, :], x[:, t, :], ACT.Square, accum_out=ssx[:, t:t + 1])
                act.drain().then_inc(tss_ready, 1)

            def rows_back(t):
                for half in range(2):
                    nc.scalar.copy(hrow[:, t, half * 512:(half + 1) * 512], take()).then_inc(pa_free, 1)

            def exponents(n, t):
                act.wait_ge(g_arg, n + 1)
                nc.scalar.activation(wexp[:, t], wexp[:, t], ACT.Exp).then_inc(g_exp, 1)

            def diagonals(tt, i0, i1):
                act.wait_ge(handed, tt + 1)
                for i in range(i0, i1):
                    q = PE_FIRST[tt] + i
                    if i >= DIAGS:
                        act.wait_ge(rows_free, taken_in(tt, q - DIAGS))
                    nc.scalar.activation(diag[:, i % DIAGS, :], ident[:, :], ACT.Copy, scale=coef[:, q:q + 1]).then_inc(diag_ready, 1)

            def gelus(tt):
                act.wait_ge(dots_ready, tt + 1)
                nc.scalar.activation(coef[:, :], dots[:, :], ACT.Gelu).then_inc(gelu_ready, 1)

            for half in range(6):
                nc.scalar.copy(grows[:, half // 2, (half % 2) * 512:(half % 2 + 1) * 512], take()).then_inc(pa_free, 1)
            act.drain().then_inc(grows_ready, 1)
            squares(0)
            act.wait_ge(if_abs, 1)
            nc.scalar.activation(ge[:, :], ge[:, :], ACT.Exp, scale=-1.0)
            act.drain()
            nc.scalar.activation(gl[:, :], ge[:, :], ACT.Ln, bias=1.0).then_inc(if_log, 1)
            for j in range(KC // 2):
                act.wait_ge(qk_pre, j + 1)
                nc.scalar.activation(qkT[:, 2 * j:2 * j + 2, :], qkT[:, 2 * j:2 * j + 2, :], ACT.Silu).then_inc(qk_silu, 1)
            for j in range(2):
                for t in range(NT):
                    nc.scalar.copy(vaug[:, t, 4 * j:4 * j + 4, 0:LSTM_V], take().rearrange("p (h v) -> p h v", v=LSTM_V)).then_inc(pa_free, 1)
            act.drain().then_inc(v_ready, 1)
            for j in range(2):
                for t in range(NT):
                    nc.scalar.activation(so[:, t, j * 512:(j + 1) * 512], take(), ACT.Sigmoid).then_inc(pa_free, 1)
            act.wait_ge(if_sum, 1)
            nc.scalar.activation(gm[:, :], gm[:, :], ACT.Exp, scale=-1.0).then_inc(if_exp, 1)
            for h in range(LSTM_HEADS + 1):
                if h < LSTM_HEADS:
                    act.wait_ge(d_pre, h + 1)
                    nc.scalar.activation(Dt[:, h % 2, :], Dt[:, h % 2, :], ACT.Exp, scale=-1.0).then_inc(d_ready, 1)
                if h:
                    nc.scalar.copy(numS[:, h - 1].rearrange("p t v -> p (t v)"), take()[:, 0:2 * (LSTM_V + 1)]).then_inc(pa_free, 1)
            act.drain().then_inc(num_ready, 1)
            columns_out(hT, yT_ready)
            experts_first()
            exponents(0, 0)
            gelus(0)
            diagonals(0, 0, PE_ROWS - TOPK)
            exponents(1, 1)
            diagonals(0, PE_ROWS - TOPK, PE_ROWS)

            def second_layer(t):
                tile_squares(t, experts_done)
                cut = slice(t * P, (t + 1) * P)
                for n, dst in enumerate((krow[:, :], vrow[:, t], qrow[:, :])):
                    for j in range(2):
                        nc.scalar.copy(dst[:, j * 512:(j + 1) * 512], take()).then_inc(pa_free, 1)
                    act.drain().then_inc(srow_ready, 1)
                for dst in (skT[:, :, cut], sqT[:, :, :]):
                    for half in range(2):
                        nc.scalar.copy(dst[:, 4 * half:4 * half + 4, :], take().rearrange("p (c n) -> p c n", n=P)).then_inc(pa_free, 1)
                act.drain().then_inc(sT_ready, 1)
                gelus(1 + t)
                groups, g0 = STICK_GROUPS[t], STICK_BEFORE[t]
                for g in range(len(groups) + 1):
                    if g < len(groups):
                        n = g0 + g
                        r = n % 2
                        act.wait_ge(z_full, n + 1)
                        nc.scalar.activation(az[:, r, :], pr[r][:, :], ACT.Abs)
                        act.drain()
                        nc.scalar.activation(az[:, r, :], az[:, r, :], ACT.Exp, scale=-1.0)
                        act.drain()
                        nc.scalar.activation(az[:, r, :], az[:, r, :], ACT.Ln, bias=1.0).then_inc(sL_ready, 1)
                    if g:
                        n = g0 + g - 1
                        act.wait_ge(ex_ready, n + 1)
                        nc.scalar.activation(ex[:, n % 2, :], ex[:, n % 2, :], ACT.Exp).then_inc(a_exp, 1)
                for half in range(2):
                    nc.scalar.copy(xn[:, t, half * 512:(half + 1) * 512], take()).then_inc(pa_free, 1)
                act.drain().then_inc(ty_rows, 1)
                for half in range(2):
                    nc.scalar.copy(hT[:, 4 * half:4 * half + 4, cut], take().rearrange("p (c n) -> p c n", n=P)).then_inc(pa_free, 1)
                act.drain().then_inc(tyT_ready, 1)
                tile_squares(t, stick_done)
                rows_back(t)
                for j in range(4):
                    nc.scalar.copy(flat(qpt[:, 4 * j:4 * j + 4, :]), take()).then_inc(pa_free, 1)
                act.drain().then_inc(qp_ready, 1)
                for j in range(4):
                    nc.scalar.copy(flat(sc[:, 4 * j:4 * j + 4, :]), take()).then_inc(pa_free, 1)
                act.drain().then_inc(sc_ready, 1)
                diagonals(1 + t, 0, PE_ROWS - TOPK)
                exponents(2 + t, t)
                diagonals(1 + t, PE_ROWS - TOPK, PE_ROWS)

            for t in range(NT):
                second_layer(t)
            gelus(3)

        @block.gpsimd
        def _(pool):
            pool.wait_ge(c_ready, 1)
            with pool.Fori(0, ADA_CHUNKS // 2) as i:
                for a in range(2):
                    pool.wait_ge(ada_free, 2 * i + a + 1)
                    pool.sem_inc(wait_seen, 1)
                    pool.dma_start(aring[:, a, :], ins["ada_rows"][bass.ds(2 * i + a, 1)].rearrange("a p n -> p (a n)")).then_inc(ada_in[a], 16)
            for tt in range(DEPTH * NT):
                for phase, table in ((2 * tt, "peer_u"), (2 * tt + 1, "peer_v")):
                    with pool.Fori(0, TURNS) as i:
                        for a in range(2):
                            pool.wait_ge(ix_ready, 8 * phase + 2 * i + a + 1)
                            pool.sem_inc(wait_seen, 1)
                            for j in range(TOPK):
                                n = a * TOPK + j
                                pool.wait_ge(rows_free, phase * PICKS + i * PAIR + n + 1)
                                pool.sem_inc(wait_seen, 1)
                                pool.indirect_dma_start(out=gring[:, n % RING, :], out_offset=None, in_=ins[table],
                                                        in_offset=bass.IndirectOffsetOnAxis(ap=ix[:, a, j:j + 1], axis=0)).then_inc(row_in[n % RING], 16)

        @block.vector
        def _(dve):
            dve.sem_inc(pd_free, 2)
            dve.sem_inc(par_free, 2)
            dve.sem_inc(sc_read, 2)
            dve.sem_inc(pt_ready, 1)
            dve.sem_inc(o_read, 1)
            dve.sem_inc(row_read, 4)
            dve.sem_inc(silu_free, 2)
            dve.wait_ge(const_in, 48)
            dve.wait_ge(x_in, 16)
            dve.sem_inc(x_ready, 1)
            dve.drain()

            def rsqrt(y, total, n, eps=EPS):
                w = total.shape[1]
                v, a = rsv[:, 0:w], rsa[:, 0:w]
                y, total = y[:, 0:w], total[:, 0:w]
                nc.vector.tensor_scalar(v, total, 1.0 / n, eps, ALU.mult, ALU.add)
                dve.drain()
                nc.vector.tensor_scalar(a.bitcast(I32), v.bitcast(I32), 1, None, ALU.arith_shift_right)
                dve.drain()
                nc.vector.tensor_scalar(y.bitcast(I32), a.bitcast(I32), -1.0, float(0x5F3759DF), ALU.mult, ALU.add)
                dve.drain()
                for _ in range(3):
                    nc.vector.scalar_tensor_tensor(a, y, -0.5, y, ALU.mult, ALU.mult)
                    dve.drain()
                    nc.vector.tensor_tensor(a, a, v, ALU.mult)
                    dve.drain()
                    nc.vector.scalar_tensor_tensor(y, a, 1.5, y, ALU.add, ALU.mult)
                    dve.drain()

            dve.sem_inc(ada_free, 2)
            dve.sem_inc(rows_free, RING)
            with dve.Fori(0, DEPTH) as l:
                nd = [0]
                nada = [0]

                def modulation(n):
                    for _ in range(n):
                        j = nada[0]
                        nada[0] += 1
                        dve.wait_ge(ada_in[j % 2], 16 * (ADA_LAYER // 2) * l + 16 * (j // 2) + 16)
                        nc.vector.tensor_tensor_reduce(out=aring[:, j % 2, :], in0=aring[:, j % 2, :], in1=crow[:, :], scale=1.0, scalar=0.0,
                                                       op0=ALU.mult, op1=ALU.add, accum_out=adal[:, j:j + 1]).then_inc(ada_free, 1)

                def take():
                    u = nd[0]
                    nd[0] += 1
                    dve.wait_ge(pd_full, l * D_UNITS + u + 1)
                    return pd[u % 2]

                def lower_parts(h):
                    dve.wait_ge(whi_ready, l * HALVES + h + 1)
                    raw, ks = raw_half(h)
                    nc.vector.tensor_tensor(wlo[:, h % 2, ks, :], raw, whi[:, h % 2, ks, :], ALU.subtract).then_inc(wlo_ready, 1)

                def norm(n, g):
                    dve.wait_ge(ss_ready, 2 * l + n + 1)
                    rsqrt(rsx, ssx, D)
                    for t in range(NT):
                        nc.vector.tensor_scalar(xn[:, t, :], x[:, t, :], rsx[:, t:t + 1], None, ALU.mult)
                    dve.drain()
                    dve.sem_inc(xn_ready, 1)
                    for j in range(KC // 2):
                        b = take()
                        gb = cols[:, g + 2 * j:g + 2 * j + 2].unsqueeze(2).to_broadcast([P, 2, SEQ])
                        nc.vector.tensor_tensor(hT[:, 2 * j:2 * j + 2, :], b[:, :].rearrange("p (c n) -> p c n", c=2), gb,
                                                ALU.mult).then_inc(pd_free, 1)
                        if n:
                            dve.drain()
                            c = slice(2 * j, 2 * j + 2)
                            nc.vector.tensor_copy(hhi[:, c, :], hT[:, c, :])
                            dve.drain()
                            nc.vector.tensor_tensor(hlo[:, c, :], hT[:, c, :], hhi[:, c, :], ALU.subtract)
                    dve.drain()
                    dve.sem_inc(hT_ready, 1)

                def add_rows(n):
                    dve.wait_ge(ssm_ready, 4 * (2 * l + n) + 4)
                    nc.vector.tensor_tensor(rsm[:, :], ssm[:, :, 0], ssm[:, :, 1], ALU.add)
                    dve.drain()
                    rsqrt(rsm, rsm, D)
                    for half in range(2):
                        for t in range(NT):
                            cut = slice(half * 512, (half + 1) * 512)
                            nc.vector.scalar_tensor_tensor(xn[:, t, cut], pr[2 * t + half][:, :], rsm[:, t:t + 1],
                                                           post_gain[:, n, cut], ALU.mult, ALU.mult).then_inc(row_read, 1)
                    dve.drain()
                    for t in range(NT):
                        nc.vector.tensor_tensor(x[:, t, :], x[:, t, :], xn[:, t, :], ALU.add)
                    dve.drain()
                    dve.sem_inc(x_ready, 1)

                nc.vector.memset(uT[:, :, 0:1], 0.0)
                nc.vector.memset(uT[:, :, SEQ + 1:SEQ + 2], 0.0)
                dve.wait_ge(par_in, 64 * l + 64)
                norm(0, G_PRE)
                modulation(12)
                dve.wait_ge(qk_ready, 2 * l + 1)
                HK = HEADS + KV_HEADS
                heads = zrow[:, :, 0:HK * HD].rearrange("p t (h d) -> p t h d", d=HD)
                x1, x2 = heads[:, :, :, 0:HALF], heads[:, :, :, HALF:ROT]
                tmp = [rt[:, i, :].rearrange("p (t h d) -> p t h d", t=NT, d=HALF) for i in range(4)]
                cosb = cs[:, 0, :, :].unsqueeze(2).to_broadcast([P, NT, HK, HALF])
                sinb = cs[:, 1, :, :].unsqueeze(2).to_broadcast([P, NT, HK, HALF])
                nc.vector.tensor_tensor(tmp[0], x1, cosb, ALU.mult)
                nc.vector.tensor_tensor(tmp[1], x2, sinb, ALU.mult)
                nc.vector.tensor_tensor(tmp[2], x2, cosb, ALU.mult)
                nc.vector.tensor_tensor(tmp[3], x1, sinb, ALU.mult)
                dve.drain()
                nc.vector.tensor_tensor(x1, tmp[0], tmp[1], ALU.subtract)
                nc.vector.tensor_tensor(x2, tmp[2], tmp[3], ALU.add)
                dve.drain()
                for t in range(NT):
                    for a in range(2):
                        nc.vector.tensor_copy(kdup[:, t, :, a, :], zrow[:, t, HEADS * HD:HK * HD].rearrange("p (g d) -> p g d", d=HD))
                dve.drain()
                dve.sem_inc(rope_done, 1)

                def values_out(g):
                    dve.wait_ge(o_full, l * HEADS + 4 * g + 4)
                    dve.wait_ge(es_ready, l * 4 + g + 1)
                    nc.vector.tensor_tensor(es[:, :, :], es[:, :, :], den[:, 4 * g:4 * g + 4, :], ALU.add)
                    dve.drain()
                    nc.vector.reciprocal(rden[:, :, :], es[:, :, :].rearrange("p h t -> p t h"))
                    dve.drain()
                    for t in range(NT):
                        nc.vector.tensor_tensor(orow[:, t, 4 * g * HD:4 * (g + 1) * HD].rearrange("p (h d) -> p h d", d=HD),
                                                po[:, t * 256:(t + 1) * 256].rearrange("p (h d) -> p h d", d=HD),
                                                rden[:, t, :].unsqueeze(2).to_broadcast([P, 4, HD]), ALU.mult)
                    dve.drain()
                    dve.sem_inc(o_read, 1)
                    dve.sem_inc(o_rows, 1)

                def softmax_max(h):
                    dve.wait_ge(sc_full, l * HEADS + h + 1)
                    dve.sem_inc(sc_seen, 1)
                    for t in range(NT):
                        nc.vector.tensor_tensor_reduce(out=S[:, h % 2, t, :], in0=psc[h % 2][:, t * SEQ:(t + 1) * SEQ],
                                                       in1=mask8[:, t, :], scale=HD ** -0.5, scalar=-3e38,
                                                       op0=ALU.add, op1=ALU.max, accum_out=rmx[:, h, t:t + 1])
                    dve.drain()
                    dve.sem_inc(sc_read, 1)
                    nc.vector.tensor_scalar(nm[:, h, :], rmx[:, h, :], sinks[:, h:h + 1], -1.0, ALU.max, ALU.mult)
                    dve.drain()
                    dve.sem_inc(nm_ready, 1)

                def probs_out(h):
                    dve.wait_ge(pt_full, l * HEADS + h + 1)
                    nc.vector.tensor_copy(PT[:, h % 2, :, :].rearrange("p t n -> p (t n)"), ppt[:, :])
                    dve.drain()
                    dve.sem_inc(pt_ready, 1)

                def conv(j):
                    b = take()
                    dve.wait_ge(cc_ready, 4 * l + j + 1)
                    nc.vector.tensor_tensor(uT[:, 2 * j:2 * j + 2, 1:SEQ + 1], b[:, :].rearrange("p (c n) -> p c n", c=2),
                                            ccT[:, 2 * j:2 * j + 2, :], ALU.mult).then_inc(pd_free, 1)
                    dve.drain()
                    for k in range(3):
                        for c in range(2):
                            cc = 2 * j + c
                            w = cols[:, CONVW + 3 * cc + k:CONVW + 3 * cc + k + 1]
                            if k == 0:
                                nc.vector.tensor_scalar(cvt[:, c, :], uT[:, cc, 0:SEQ], w, None, ALU.mult)
                            else:
                                nc.vector.scalar_tensor_tensor(cvt[:, c, :], uT[:, cc, k:k + SEQ], w, cvt[:, c, :], ALU.mult, ALU.add)
                        dve.drain()
                    nc.vector.tensor_tensor(cbT[:, 2 * j:2 * j + 2, :], cbT[:, 2 * j:2 * j + 2, :], cvt[:, :, :], ALU.mult)
                    dve.drain()

                for s in range(16):
                    if s >= 4:
                        modulation(1)
                    if 4 <= s < 8:
                        conv(s - 4)
                    if s == 8:
                        dve.sem_inc(yconv_ready, 1)
                    if s >= 2 and (s - 2) % 4 == 3:
                        values_out((s - 2) // 4)
                    if s >= 1:
                        probs_out(s - 1)
                    softmax_max(s)
                    if s % 4 == 3:
                        nc.vector.tensor_tensor(es[:, :, :], nm[:, s - 3:s + 1, :], sinks[:, s - 3:s + 1].unsqueeze(2).to_broadcast([P, 4, NT]), ALU.add)
                        dve.drain()
                        dve.sem_inc(es_sum, 1)
                for j in range(4):
                    b = take()
                    if j == 0:
                        dve.wait_ge(sig_ready, l + 1)
                    v = sgb[:, 2 * j:2 * j + 2, :].rearrange("p c n -> p (c n)")
                    nc.vector.tensor_tensor(v, b[:, :], v, ALU.mult).then_inc(pd_free, 1)
                    if j == 0:
                        probs_out(HEADS - 1)
                values_out(3)
                for j in range(4):
                    b = take()
                    v = sga[:, 2 * j:2 * j + 2, :].rearrange("p c n -> p (c n)")
                    w = sgb[:, 2 * j:2 * j + 2, :].rearrange("p c n -> p (c n)")
                    nc.vector.tensor_tensor(v, b[:, :], v, ALU.mult).then_inc(pd_free, 1)
                    dve.drain()
                    nc.vector.tensor_tensor(v, v, w, ALU.add)
                dve.drain()
                dve.sem_inc(mix_ready, 1)
                lower_parts(0)
                lower_parts(1)
                add_rows(0)
                norm(1, G_FFN)
                for u in range(FC):
                    if u % 2 == 0:
                        lower_parts(u + 2)
                    b = take()
                    dve.wait_ge(silu_ready, l * FC + u + 1)
                    f = hT[:, u % 2, :]
                    nc.vector.tensor_tensor(f, b[:, SEQ:2 * SEQ], silu[:, u % 2, :], ALU.mult).then_inc(pd_free, 1)
                    dve.drain()
                    dve.sem_inc(silu_free, 1)
                    nc.vector.tensor_copy(fhi[:, u, :], f)
                    dve.drain()
                    nc.vector.tensor_tensor(flo(u), f, fhi[:, u, :], ALU.subtract)
                    if u % 2:
                        lower_parts(u + 2)
                    modulation(1)
                dve.drain()
                dve.sem_inc(f_ready, 1)
                for h in range(FC + 2, HALVES):
                    lower_parts(h)
                    modulation(1)
                add_rows(1)
                dve.sem_inc(par_free, 2)
                nc.vector.tensor_copy(adac[:, bass.ds(l * ADA_LAYER, ADA_LAYER)], adal[:, :])
                dve.drain()
                assert (nd[0], nada[0]) == (D_UNITS, ADA_LAYER)

            nd = [DEPTH * D_UNITS]

            def take():
                u = nd[0]
                nd[0] += 1
                dve.wait_ge(pd_full, u + 1)
                return pd[u % 2]

            dve.wait_ge(cols2_in, 32)
            nc.vector.tensor_tensor(adac[:, :], adac[:, :], adab[:, :], ALU.add)
            dve.drain()

            def shift(n):
                c = KV_ADA if n == 4 else ((n // 2) * 6 + 3 * (n % 2)) * KC
                return adac[:, c:c + KC]

            for n in range(5):
                c = KV_ADA + KC if n == 4 else ((n // 2) * 6 + 3 * (n % 2) + 1) * KC
                g = N_KV if n == 4 else (N_MIX, N_FFN)[n % 2] + (n // 2) * KC
                nc.vector.scalar_tensor_tensor(modA[:, n, :], adac[:, c:c + KC], 1.0, cols2[:, g:g + KC], ALU.add, ALU.mult)
            dve.drain()
            dve.sem_inc(mod_ready, 1)

            def norm(n, outs):
                dve.wait_ge(ss_ready, 2 * DEPTH + n + 1)
                rsqrt(rsx, ssx, D)
                for t in range(NT):
                    nc.vector.tensor_scalar(xn[:, t, :], x[:, t, :], rsx[:, t:t + 1], None, ALU.mult)
                dve.drain()
                dve.sem_inc(xn_ready, 1)
                for j in range(KC // 2):
                    b = take()
                    for m, dst in outs:
                        for i in range(2):
                            c = 2 * j + i
                            nc.vector.tensor_scalar(dst[:, c, :], b[:, i * SEQ:(i + 1) * SEQ], modA[:, m, c:c + 1], shift(m)[:, c:c + 1],
                                                    ALU.mult, ALU.add)
                    dve.drain()
                    dve.sem_inc(pd_free, 1)
                dve.sem_inc(hT_ready, 1)

            def add_gated(t, g, between, done):
                for half in range(2):
                    c = slice(half * 512, (half + 1) * 512)
                    b = take()
                    nc.vector.tensor_tensor(xn[:, t, c], b[:, :], grows[:, g, c], ALU.mult).then_inc(pd_free, 1)
                    between(3)
                dve.drain()
                nc.vector.tensor_tensor(x[:, t, :], x[:, t, :], xn[:, t, :], ALU.add)
                dve.drain()
                dve.sem_inc(done, 1)

            def tile_norm(t, k, outs, between=lambda n: None):
                dve.wait_ge(tss_ready, k + 1)
                rsqrt(rsx[:, t:t + 1], ssx[:, t:t + 1], D)
                nc.vector.tensor_scalar(xn[:, t, :], x[:, t, :], rsx[:, t:t + 1], None, ALU.mult)
                dve.drain()
                dve.sem_inc(txn_ready, 1)
                between(3)
                for half in range(2):
                    b = take()
                    for m, dst in outs:
                        for i in range(4):
                            c = 4 * half + i
                            nc.vector.tensor_scalar(dst[:, c, :], b[:, i * P:(i + 1) * P], modA[:, m, c:c + 1], shift(m)[:, c:c + 1],
                                                    ALU.mult, ALU.add)
                    dve.drain()
                    dve.sem_inc(pd_free, 1)
                    between(2)
                dve.sem_inc(thT_ready, 1)

            def head_norm(v, sq, ss, rs, gain, n, scale):
                nc.vector.tensor_tensor(sq, v, v, ALU.mult)
                dve.drain()
                nc.vector.tensor_reduce(ss, sq.rearrange("p (h d) -> p h d", d=n), AX.X, ALU.add)
                dve.drain()
                rsqrt(rs, ss, n)
                v3 = v.rearrange("p (h d) -> p h d", d=n)
                nc.vector.tensor_tensor(v3, v3, rs.unsqueeze(2).to_broadcast([P, rs.shape[1], n]), ALU.mult)
                dve.drain()

            norm(0, [(0, hT)])
            dve.wait_ge(lstm_in, 64)
            nc.vector.memset(preT[:, :, 0:LSTM_CONV - 1], 0.0)
            nc.vector.memset(vaug[:, :, :, LSTM_V:LSTM_V + 1], 1.0)
            nc.vector.memset(gone[:, :], 1.0)
            for j in range(KC // 2):
                b = take()
                nc.vector.tensor_copy(preT[:, 2 * j:2 * j + 2, LSTM_CONV - 1:], b[:, :].rearrange("p (c n) -> p c n", c=2)).then_inc(pd_free, 1)
            dve.drain()
            dve.wait_ge(if_full, 1)
            nc.vector.tensor_scalar(gi[:, :], pr[0][0:LSTM_HEADS, 0:SEQ], bif[:, 0:1], None, ALU.add)
            nc.vector.tensor_scalar(gf[:, :], pr[0][0:LSTM_HEADS, SEQ:2 * SEQ], bif[:, 1:2], None, ALU.add)
            dve.drain()
            nc.vector.scalar_tensor_tensor(ge[:, :], gf[:, :], -1.0, gf[:, :], ALU.mult, ALU.max)
            dve.drain()
            dve.sem_inc(if_abs, 1)
            for j in range(KC // 2):
                for k in range(LSTM_CONV):
                    for c in range(2):
                        cc = 2 * j + c
                        w = cols2[:, LCONV + LSTM_CONV * cc + k:LCONV + LSTM_CONV * cc + k + 1]
                        dst = qkT[:, cc, :] if k == LSTM_CONV - 1 else lcv[:, c, :]
                        if k == 0:
                            nc.vector.tensor_scalar(dst, preT[:, cc, 0:SEQ], w, None, ALU.mult)
                        else:
                            nc.vector.scalar_tensor_tensor(dst, preT[:, cc, k:k + SEQ], w, lcv[:, c, :], ALU.mult, ALU.add)
                    dve.drain()
                dve.sem_inc(qk_pre, 1)
            dve.wait_ge(if_log, 1)
            nc.vector.scalar_tensor_tensor(gf[:, :], gf[:, :], 0.0, gl[:, :], ALU.min, ALU.subtract)
            dve.drain()
            nc.vector.tensor_tensor_scan(gb_[:, :], gone[:, :], gf[:, :], 0.0, ALU.mult, ALU.add)
            dve.drain()
            nc.vector.tensor_tensor(gg[:, :], gi[:, :], gb_[:, :], ALU.subtract)
            dve.drain()
            nc.vector.tensor_tensor_scan(gM[:, :], gg[:, :], gg[:, :], 0.0, ALU.max, ALU.max)
            dve.drain()
            nc.vector.tensor_tensor(gm[:, :], gb_[:, :], gM[:, :], ALU.add)
            dve.drain()
            dve.sem_inc(if_sum, 1)
            dve.wait_ge(gcol_full, 1)
            nc.vector.tensor_copy(gcol[:, :, :].rearrange("p a h -> p (a h)"), pr[1][:, 0:4 * LSTM_HEADS])
            dve.drain()
            dve.sem_inc(gcol_ready, 1)
            for h in range(LSTM_HEADS):
                dve.wait_ge(m_full, h + 1)
                for s_, (a0, a1, m0) in enumerate(((0, SEQ, 0), (SEQ, 3 * P, P))):
                    nc.vector.scalar_tensor_tensor(Dt[:, h % 2, a0:a1], pr[h % 2][:, m0:SEQ], gcol[:, s_, h:h + 1], biglm[:, a0:a1],
                                                   ALU.subtract, ALU.max)
                dve.drain()
                dve.sem_inc(d_pre, 1)
                dve.sem_inc(m_read, 1)
                dve.wait_ge(d_ready, h + 1)
                dve.wait_ge(st_full, h + 1)
                nc.vector.scalar_tensor_tensor(Pl[:, h % 2, :], pr[2 + h % 2][:, 0:3 * P], LSTM_QK ** -0.5, Dt[:, h % 2, :], ALU.mult, ALU.mult)
                dve.drain()
                dve.sem_inc(st_read, 1)
                dve.sem_inc(pl_ready, 1)
            dve.wait_ge(num_ready, 1)
            nc.vector.scalar_tensor_tensor(dcol[:, :, :], numS[:, :, :, LSTM_V], -1.0, numS[:, :, :, LSTM_V], ALU.mult, ALU.max)
            dve.drain()
            nc.vector.tensor_tensor(dcol[:, :, :], dcol[:, :, :], gcol[:, 2:4, :].rearrange("p t h -> p h t"), ALU.max)
            dve.drain()
            nc.vector.reciprocal(dcol[:, :, :], dcol[:, :, :])
            dve.drain()
            for t in range(NT):
                nc.vector.tensor_tensor(xn[:, t, :].rearrange("p (h v) -> p h v", v=LSTM_V), numS[:, :, t, 0:LSTM_V],
                                        dcol[:, :, t].unsqueeze(2).to_broadcast([P, LSTM_HEADS, LSTM_V]), ALU.mult)
            dve.drain()
            flat_xn = xn[:, :, :].rearrange("p t n -> p (t n)")
            head_norm(flat_xn, numS[:, :, :, :].rearrange("p h t v -> p (h t v)")[:, 0:NT * D], rsb[:, 0:16], rcol[:, :], None, LSTM_V, 1.0)
            nc.vector.tensor_tensor(xn[:, :, :], xn[:, :, :], hng[:, :].unsqueeze(1).to_broadcast([P, NT, D]), ALU.mult)
            dve.drain()
            nc.vector.tensor_tensor(xn[:, :, :], xn[:, :, :], so[:, :, :], ALU.mult)
            dve.drain()
            dve.sem_inc(y_rows, 1)
            dve.wait_ge(grows_ready, 1)
            for t in range(NT):
                add_gated(t, 0, lambda n: None, mixed)
            for t in range(NT):
                tile_norm(t, t, [(1, hT[:, :, t * P:(t + 1) * P])])

            def top16(src, spare, vals, idxs, n, spread):
                for i in range(n):
                    nc.vector.max(vals(i)[:, 0:8], src(i))
                dve.drain()
                spread()
                for i in range(n):
                    nc.vector.max_index(idxs(i)[:, 0:8], vals(i)[:, 0:8], src(i))
                    nc.vector.match_replace(spare(i), vals(i)[:, 0:8], src(i), -3e38)
                dve.drain()
                spread()
                for i in range(n):
                    nc.vector.max(vals(i)[:, 8:16], spare(i))
                dve.drain()
                spread()
                for i in range(n):
                    nc.vector.max_index(idxs(i)[:, 8:16], vals(i)[:, 8:16], spare(i))
                dve.drain()
                spread()

            def choose(l, t, spread=lambda: None):
                sc = (scores_0, sc1)[t] if l == 0 else scores_0
                dve.wait_ge(sc_ready, NT * l + t + 1)
                top16(lambda i: sc[:, i, :], lambda i: sc2[:, i, :], lambda i: top[:, i // 2, i % 2, :],
                      lambda i: topi[:, i // 2, i % 2, :], 2 * PEER_HEADS, spread)
                nc.vector.tensor_copy(topf[:, :, :, :], topi[:, :, :, :])
                shape = [P, PEER_HEADS, TOPK, TOPK]
                c4 = cand[:, :, :].rearrange("p h (i j) -> p h i j", j=TOPK)
                nc.vector.tensor_tensor(c4, top[:, :, 0, :].unsqueeze(3).to_broadcast(shape), top[:, :, 1, :].unsqueeze(2).to_broadcast(shape), ALU.add)
                dve.drain()
                pick = scores_0[:, :, :].rearrange("p (h a) n -> p h (a n)", a=2)
                spare = sc2[:, :, :].rearrange("p (h a) n -> p h (a n)", a=2)
                top16(lambda i: cand[:, i, :], lambda i: spare[:, i, :], lambda i: gt[:, i, :], lambda i: pos[:, i, :], PEER_HEADS, spread)
                nc.vector.tensor_tensor(wexp[:, t], gt[:, :, :], gt[:, :, 0:1].to_broadcast([P, PEER_HEADS, TOPK]), ALU.subtract)
                dve.drain()
                dve.sem_inc(g_arg, 1)
                pf = pos[:, :, :].rearrange("p h k -> p (h k)")
                nc.vector.tensor_scalar(hilo[:, 0, :], pf, 4, None, ALU.logical_shift_right)
                nc.vector.tensor_scalar(hilo[:, 1, :], pf, 15, None, ALU.bitwise_and)
                dve.drain()
                nc.vector.tensor_copy(hilof[:, :, :], hilo[:, :, :])
                dve.drain()
                for a in range(2):
                    p3 = pick.rearrange("p h (k i) -> p (h k) i", i=TOPK)
                    p4 = pick.rearrange("p h (k i) -> p h k i", i=TOPK)
                    nc.vector.tensor_tensor(p3, hilof[:, a, :].unsqueeze(2).to_broadcast([P, PICKS, TOPK]),
                                            iota[:, :].unsqueeze(1).to_broadcast([P, PICKS, TOPK]), ALU.is_equal)
                    dve.drain()
                    nc.vector.tensor_tensor(p4, p4, topf[:, :, a, :].unsqueeze(2).to_broadcast(shape), ALU.mult)
                    dve.drain()
                    nc.vector.tensor_reduce(ef[:, a, :], p3, AX.X, ALU.add)
                    dve.drain()
                    spread()
                nc.vector.tensor_scalar(ef[:, 0, :], ef[:, 0, :], float(NKEYS), float(l * EXPERTS), ALU.mult, ALU.add)
                dve.drain()
                nc.vector.tensor_tensor(eidx[:, t, 0:PICKS], ef[:, 0, :], ef[:, 1, :], ALU.add)
                dve.drain()
                nc.vector.tensor_copy(eidx[:, t, PICKS:PICKS + PAIR], eidx[:, t, 0:PAIR])
                spread()
                dve.wait_ge(g_exp, 2 * l + t + 1)
                nc.vector.tensor_reduce(wsum[:, :], wexp[:, t], AX.X, ALU.add)
                dve.drain()
                nc.vector.reciprocal(wsum[:, :], wsum[:, :])
                dve.drain()
                nc.vector.tensor_tensor(wexp[:, t], wexp[:, t], wsum[:, :].unsqueeze(2).to_broadcast([P, PEER_HEADS, TOPK]), ALU.mult)
                dve.drain()
                dve.sem_inc(chosen, 1)

            scores_0 = sc

            def landed_row(phase, i, n):
                dve.wait_ge(row_in[n % RING], 16 * (PICKS // RING) * phase + i * (16 * PAIR // RING) + 16 * (n // RING + 1))

            def next_picks(a, src):
                nc.vector.tensor_copy(ix[:, a, :], src)
                dve.drain()
                dve.sem_inc(ix_ready, 1)

            def up_row(t, n, a, j):
                nc.vector.tensor_tensor_reduce(out=gring[:, n % RING, :], in0=gring[:, n % RING, :], in1=hrow[:, t, :], scale=1.0,
                                               scalar=0.0, op0=ALU.mult, op1=ALU.add, accum_out=a16[:, a, j:j + 1]).then_inc(rows_free, 1)

            def down_row(n, c):
                nc.vector.scalar_tensor_tensor(acc[:, :], gring[:, n % RING, :], c, acc[:, :], ALU.mult, ALU.add).then_inc(rows_free, 1)
                dve.drain()

            def up_loop(tt):
                t = tt % NT
                with dve.Fori(0, TURNS) as i:
                    for a in range(2):
                        for j in range(TOPK):
                            n = a * TOPK + j
                            landed_row(2 * tt, i, n)
                            up_row(t, n, a, j)
                        dve.drain()
                        nc.vector.tensor_copy(dots[:, bass.ds(i * PAIR + a * TOPK, TOPK)], a16[:, a, :])
                        next_picks(a, eidx[:, t, bass.ds(i * PAIR + PAIR + a * TOPK, TOPK)])

            def down_loop(tt):
                t = tt % NT
                with dve.Fori(0, TURNS) as i:
                    for a in range(2):
                        for j in range(TOPK):
                            n = a * TOPK + j
                            landed_row(2 * tt + 1, i, n)
                            down_row(n, coef[:, bass.ds(i * PAIR + n, 1)])
                        next_picks(a, eidx[:, t, bass.ds(i * PAIR + PAIR + a * TOPK, TOPK)])

            def weigh(tt):
                dve.drain()
                dve.sem_inc(dots_ready, 1)
                nc.vector.memset(acc[:, :], 0.0)
                dve.wait_ge(gelu_ready, tt + 1)
                nc.vector.tensor_tensor(coef[:, :], coef[:, :], wexp[:, tt % NT].rearrange("p h k -> p (h k)"), ALU.mult)
                dve.drain()

            def hand_over(tt):
                dve.drain()
                dve.sem_inc(handed, 1)
                calls, g0 = [0], (PICKS + PE_FIRST[tt]) // TOPK

                def between():
                    calls[0] += 1
                    for i in range(PE_ROWS // TOPK - 1):
                        if calls[0] == 3 + 4 * i and g0 + i + 2 < 2 * PEER_HEADS:
                            group_taken_in(tt, g0 + i)
                return between

            def group_taken_in(tt, g):
                dve.wait_ge(rows_free, taken_in(tt, (g + 1) * TOPK - 1 - PICKS))
                m = g + 2
                if m < 2 * PEER_HEADS:
                    next_picks(g % 2, eidx[:, tt % NT, (m - PEER_HEADS) * TOPK:(m - PEER_HEADS + 1) * TOPK])
                else:
                    m -= 2 * PEER_HEADS
                    next_picks(g % 2, eidx[:, (tt + 1) % NT, m * TOPK:(m + 1) * TOPK])

            def add_sums(tt):
                dve.wait_ge(sums_full, tt + 1)
                for half in range(2):
                    c = slice(half * 512, (half + 1) * 512)
                    nc.vector.tensor_tensor(acc[:, c], acc[:, c], pr[half][:, :], ALU.add)
                dve.drain()

            def finish(tt):
                t = tt % NT
                nc.vector.tensor_tensor(acc[:, :], acc[:, :], grows[:, 1 + tt // NT, :], ALU.mult)
                dve.drain()
                nc.vector.tensor_tensor(x[:, t, :], x[:, t, :], acc[:, :], ALU.add)
                dve.drain()
                dve.sem_inc(experts_done, 1)

            taken = [0]

            def rows_of(tt):
                t = tt % NT

                def rows(n):
                    for _ in range(min(n, PICKS - taken[0] % PICKS if taken[0] % PICKS else (PICKS if not full[0] else 0))):
                        p = taken[0]
                        phase, q = 2 * tt + p // PICKS, p % PICKS
                        g, j = p // TOPK, p % TOPK
                        landed_row(phase, q // PAIR, q % PAIR)
                        if p < PICKS:
                            up_row(t, q % PAIR, g % 2, j)
                        else:
                            down_row(q % PAIR, coef[:, q:q + 1])
                        if j == TOPK - 1:
                            if p < PICKS:
                                dve.drain()
                                nc.vector.tensor_copy(dots[:, g * TOPK:(g + 1) * TOPK], a16[:, g % 2, :])
                            m = g + 2
                            if m < 2 * PICKS // TOPK:
                                next_picks(g % 2, eidx[:, t, (m % PEER_HEADS) * TOPK:(m % PEER_HEADS + 1) * TOPK])
                            elif tt + 1 < DEPTH * NT:
                                m -= 2 * PICKS // TOPK
                                next_picks(g % 2, eidx[:, (tt + 1) % NT, m * TOPK:(m + 1) * TOPK])
                        taken[0] += 1
                        full[0] = taken[0] % PICKS == 0
                return rows

            full = [False]

            choose(0, 0)
            for a in range(2):
                next_picks(a, eidx[:, 0, a * TOPK:(a + 1) * TOPK])
            up_loop(0)
            weigh(0)
            choose(0, 1, hand_over(0))
            group_taken_in(0, PEER_HEADS + PE_ROWS // TOPK - 1)
            add_sums(0)
            taken[0], full[0] = PICKS + PE_ROWS, False
            rows = rows_of(0)
            rows(PICKS)
            finish(0)

            def second_layer(t):
                tt = 1 + t
                rows = rows_of(tt)
                taken[0], full[0] = 0, False
                cut = slice(t * P, (t + 1) * P)

                def heads_normed(v, n, scale):
                    v3 = v.rearrange("p (h d) -> p h d", d=SB_DIM)
                    head_norm(v, az[:, :, :].rearrange("p a n -> p (a n)"), sss[:, :], srs[:, :], None, SB_DIM, 1.0)
                    nc.vector.scalar_tensor_tensor(v3, v3, scale, qkg[:, n, :].unsqueeze(1).to_broadcast([P, SB_HEADS, SB_DIM]), ALU.mult, ALU.mult)
                    dve.drain()
                    dve.sem_inc(sqk_ready, 1)

                rows(4)
                tile_norm(t, NT + 2 * t, [(4, hkT[:, :, :]), (2, hT[:, :, cut])], rows)
                rows(20)
                dve.wait_ge(stick_in, 96)
                dve.wait_ge(srow_ready, 3 * t + 1)
                heads_normed(krow[:, :], 0, 1.0)
                rows(40)
                dve.wait_ge(srow_ready, 3 * t + 3)
                heads_normed(qrow[:, :], 1, SB_DIM ** -0.5)
                rows(PICKS)
                weigh(tt)
                full[0] = False

                groups, g0, ks = STICK_GROUPS[t], STICK_BEFORE[t], t + 1

                def masked(v):
                    d = v.rearrange("p (i s n) -> p i s n", s=ks, n=P)[:, :, ks - 1, :]
                    nc.vector.tensor_tensor(d, d, before[:, :].unsqueeze(1).to_broadcast([P, len(groups[0]), P]), ALU.mult)
                    dve.drain()

                share = 3 if t == 0 else 2
                for g in range(len(groups) + 1):
                    if g < len(groups):
                        n = g0 + g
                        r, z = n % 2, pr[n % 2][:, :]
                        dve.wait_ge(sL_ready, n + 1)
                        nc.vector.scalar_tensor_tensor(sp_[:, r, :], z, 0.0, az[:, r, :], ALU.max, ALU.add)
                        nc.vector.scalar_tensor_tensor(ls[:, r, :], z, 0.0, az[:, r, :], ALU.min, ALU.subtract)
                        dve.drain()
                        dve.sem_inc(z_read, 1)
                        masked(sp_[:, r, :])
                        dve.sem_inc(spm_ready, 1)
                    if g >= 1:
                        n = g0 + g - 1
                        r = n % 2
                        dve.wait_ge(cum_full, n + 1)
                        if g - 1 >= 2:
                            k = g - 3
                            if k == len(groups) // 2 - 1:
                                dve.wait_ge(pa_full, STICK_FULL[t])
                            else:
                                dve.wait_ge(a_used, (len(STICK_GROUPS[0]) - 2) * t + k + 1 - (k >= len(groups) // 2))
                        nc.vector.tensor_tensor(ex[:, r, :], ls[:, r, :], pr[2 + r][:, :], ALU.subtract)
                        dve.drain()
                        dve.sem_inc(cum_read, 1)
                        dve.sem_inc(ex_ready, 1)
                        rows(share)
                        dve.wait_ge(a_exp, n + 1)
                        masked(ex[:, r, :])
                        dve.sem_inc(a_ready, 1)
                    rows(share)
                rows(8)
                add_gated(t, 0, rows, stick_done)
                rows(2)
                tile_norm(t, NT + 2 * t + 1, [(3, hT[:, :, cut])], rows)
                assert taken[0] <= 2 * PICKS - PE_ROWS
                rows(2 * PICKS - PE_ROWS - taken[0])
                choose(1, t, hand_over(tt))
                group_taken_in(tt, 2 * PEER_HEADS - 2)
                group_taken_in(tt, 2 * PEER_HEADS - 1)
                add_sums(tt)
                finish(tt)

            for t in range(NT):
                second_layer(t)
            up_loop(3)
            weigh(3)
            down_loop(3)
            finish(3)


def tables():
    q = np.arange(SEQ)
    far = np.abs(q[:, None] - q[None, :]) > WINDOW
    mask8 = np.where(far, np.float32(NEG / HD ** -0.5), np.float32(0.0)).astype(np.float32)
    i = np.arange(P)
    big = np.where(i[:, None] <= i[None, :], np.float32(0.0), np.float32(-NEG)).astype(np.float32)
    before = (i[:, None] < i[None, :]).astype(np.float32)
    inv = np.power(np.float32(THETA), -np.arange(0, ROT, 2, dtype=np.float32) / np.float32(ROT)).astype(np.float32)
    ang = np.arange(SEQ, dtype=np.float32)[:, None] * inv[None, :]
    cs = np.stack([np.cos(ang), np.sin(ang)]).astype(np.float32)
    return {
        "c_ident": np.eye(P, dtype=np.float32),
        "c_biglm": np.concatenate([big, np.zeros((P, P), np.float32), big], axis=1),
        "c_before": before,
        "c_tri": (i[:, None] > i[None, :]).astype(np.float32),
        "c_ones": np.ones((P, P), np.float32),
        "c_iota": np.tile(np.arange(TOPK, dtype=np.float32), (P, 1)),
        "c_mask8": np.ascontiguousarray(mask8.reshape(NT, P, SEQ).transpose(1, 0, 2)),
        "c_cs": np.ascontiguousarray(cs.reshape(2, NT, P, HALF).transpose(2, 0, 1, 3)),
    }


def columns(a):
    return a.reshape(a.shape[:-1] + (-1, P)).swapaxes(-1, -2)


AS_THEY_COME = ["x", "w_in", "attn_sink", "w_attn_proj", "w_conv_proj", "w_out", "g_post_mix",
                "w_gate", "w_up", "w_down", "g_post_ffn", "c_2", "ma_w_in_2", "ma_w_out_2", "kv_w_2", "k_norm_g_2",
                "sb_w_q_2", "sb_q_norm_g_2", "sb_w_out_2", "peer_w_q_2"]


def kernel(**inputs):
    import concourse.bacc as bacc
    from concourse.bass_utils import run_bass_kernel_spmd as run

    a = {k: np.asarray(v) for k, v in inputs.items()}
    sent = {k: a[k] for k in AS_THEY_COME}
    conv = a["conv_w"].reshape(DEPTH, 3, KC, P).transpose(0, 3, 2, 1).reshape(DEPTH, P, KC * 3)
    sent["cols_a"] = np.concatenate([columns(a["g_pre_mix"]), columns(a["g_pre_ffn"]), conv], axis=2)
    lconv = a["ma_conv_w_2"][0].reshape(LSTM_CONV, KC, P).transpose(2, 1, 0).reshape(P, KC * LSTM_CONV)
    sent["cols_b"] = np.concatenate([columns(a["norm_mix_g_2"].reshape(-1)), columns(a["norm_ffn_g_2"].reshape(-1)),
                                     columns(a["kv_norm_g_2"]), lconv], axis=1)
    sent["ada_bias"] = columns(np.concatenate([a["ada_b_2"].reshape(-1), a["kv_ada_b_2"]]))
    sent["ada_rows"] = np.concatenate([a["ada_w_2"].transpose(0, 2, 1).reshape(-1, P, D), a["kv_ada_w_2"].T.reshape(-1, P, D)])
    sent["b_if"] = a["ma_b_if_2"].reshape(2, LSTM_HEADS).T
    sent["hnorm"] = a["ma_hnorm_g_2"].reshape(1, D)
    sent["keysT"] = a["peer_sub_keys_2"].transpose(0, 3, 1, 2)
    sent["peer_u"] = a["peer_u_2"].reshape(DEPTH * EXPERTS, D)
    sent["peer_v"] = a["peer_v_2"].reshape(DEPTH * EXPERTS, D)
    sent.update(tables())
    nc = bacc.Bacc("TRN2", target_bir_lowering=False, num_devices=1)
    arrays, ins = {}, {}
    for name, v in sent.items():
        arrays[f"in_{name}"] = np.ascontiguousarray(v)
        ins[name] = nc.dram_tensor(f"in_{name}", v.shape, mybir.dt.from_np(v.dtype), kind="ExternalInput").ap()
    out = nc.dram_tensor("out_0", (1, SEQ, D), F32, kind="ExternalOutput").ap()
    build(nc, ins, out)
    return run(nc, [arrays], core_ids=[0]).results[0]["out_0"]
```
